# Optimizing a Trainium2 kernel written in Bass

```python
import jax, jax.numpy as jnp
from jax import lax
import numpy as np
import math

D_MODEL = 2048
BATCH = 1
SEQ = 256
DEPTH = 1

GRID_W = 64
CTX_LEN = 256
EPS = 1e-6

A_WIDTH = D_MODEL // 2
A_HEAD = 64
A_HEADS = A_WIDTH // A_HEAD
A_DECAY_RANK = 64
A_ICLR_RANK = 64
A_LN_EPS = 64e-5

B_WIDTH = D_MODEL // 2
B_HEADS = 4
B_KEY = B_WIDTH // 2
B_DK = B_KEY // B_HEADS
B_DV = B_WIDTH // B_HEADS
B_GATE_RANK = 16
B_GATE_NORM = 16.0
B_CHUNK = 64

IN_SIZES = (3 * A_WIDTH, A_WIDTH, 2 * A_DECAY_RANK, 2 * A_ICLR_RANK,
            B_KEY, B_KEY, B_WIDTH, B_WIDTH, 2 * B_GATE_RANK, D_MODEL, D_MODEL)
P_IN = 3 * A_WIDTH + A_WIDTH + 2 * A_DECAY_RANK + 2 * A_ICLR_RANK + 2 * B_KEY + 2 * B_WIDTH + 2 * B_GATE_RANK + 2 * D_MODEL


def _rmsnorm(x, g):
    xf = x.astype(jnp.float32)
    y = xf * lax.rsqrt(jnp.mean(xf * xf, axis=-1, keepdims=True) + EPS)
    return (y * g).astype(x.dtype)

def _modulation(cond, w_mod, b_mod):
    m = jax.nn.silu(cond) @ w_mod + b_mod
    return jnp.split(m, 3, axis=-1)

def _split_points():
    return [int(s) for s in np.cumsum(IN_SIZES)[:-1]]

def _grid_conv(u, w):
    bsz, t, ch = u.shape
    rows = t // GRID_W
    img = u.reshape(bsz, rows, GRID_W, ch)
    out = lax.conv_general_dilated(img, w[:, :, None, :], (1, 1), "SAME",
                                   dimension_numbers=("NHWC", "HWIO", "NHWC"),
                                   feature_group_count=ch)
    return out.reshape(bsz, t, ch)

def _seq_conv(u, w_row):
    up = jnp.pad(u, ((0, 0), (1, 1), (0, 0)))
    return up[:, :-2] * w_row[0] + up[:, 1:-1] * w_row[1] + up[:, 2:] * w_row[2]

def _features(h, lp, grid):
    f32 = jnp.float32
    bsz, t, _ = h.shape
    p = h @ lp["w_in"]
    (rkv, z_a, lora_w, lora_a, q_b, k_b, v_b, z_b, lora_g, g_a, g_b) = jnp.split(p, _split_points(), axis=-1)
    rkv = _grid_conv(rkv, lp["conv_w"]) if grid else _seq_conv(rkv, lp["conv_w"][1])
    r, k, v = jnp.split(rkv.astype(f32), 3, axis=-1)
    lw = jnp.tanh(lora_w.astype(f32).reshape(bsz, t, 2, A_DECAY_RANK))
    w_log = lp["a_w0"] + jnp.einsum("btdr,drc->btdc", lw, lp["a_w2"])
    decay = jnp.exp(-jnp.exp(-jax.nn.softplus(-w_log) - 0.5))
    la = lora_a.astype(f32).reshape(bsz, t, 2, A_ICLR_RANK)
    iclr = jax.nn.sigmoid(lp["a_a0"] + jnp.einsum("btdr,drc->btdc", la, lp["a_a2"]))
    kk = (k * lp["a_k_k"]).reshape(bsz, t, A_HEADS, A_HEAD)
    kk = kk * lax.rsqrt(jnp.sum(kk * kk, axis=-1, keepdims=True) + 1e-12)
    k_dir = k[:, :, None, :] * (1.0 + (iclr - 1.0) * lp["a_k_a"])
    heads_a = lambda z: z.reshape(z.shape[:-1] + (A_HEADS, A_HEAD))
    gk = jnp.einsum("btdr,drc->btdc", lora_g.astype(f32).reshape(bsz, t, 2, B_GATE_RANK), lp["b_gk_w2"])
    gk = jax.nn.log_sigmoid(gk + lp["b_gk_b"]) / B_GATE_NORM
    return {
        "r": heads_a(r), "v": heads_a(v), "kk": kk, "k": heads_a(k_dir),
        "decay": heads_a(decay), "iclr": heads_a(iclr), "z_a": z_a,
        "q": q_b.astype(f32).reshape(bsz, t, B_HEADS, B_DK) * (B_DK ** -0.5),
        "kg": k_b.astype(f32).reshape(bsz, t, B_HEADS, B_DK),
        "vg": v_b.astype(f32).reshape(bsz, t, B_HEADS, B_DV),
        "gk": gk.reshape(bsz, t, 2, B_HEADS, B_DK), "z_b": z_b, "g_a": g_a, "g_b": g_b,
    }

def _rwkv_scan(r, decay, k, v, a_vec, b_vec, s0, reverse, emit):
    def step(s, inp):
        w_t, k_t, v_t, a_t, b_t = inp[:5]
        sa = jnp.einsum("bhvk,bhk->bhv", s, a_t)
        s = s * w_t[:, :, None, :] + sa[..., None] * b_t[:, :, None, :] + v_t[..., None] * k_t[:, :, None, :]
        y = jnp.einsum("bhvk,bhk->bhv", s, inp[5]) if emit else None
        return s, y
    seqs = (decay, k, v, a_vec, b_vec) + ((r,) if emit else ())
    xs = tuple(jnp.moveaxis(z, 1, 0) for z in seqs)
    s, ys = lax.scan(step, s0, xs, reverse=reverse)
    return s, (jnp.moveaxis(ys, 0, 1) if emit else None)

def _gla_chunked(q, k, v, g, s0, emit):
    bsz, t, nh, dk = q.shape
    dv = v.shape[-1]
    n = t // B_CHUNK
    chunks = lambda z: z.reshape(bsz, n, B_CHUNK, nh, z.shape[-1])
    qc, kc, vc, gc = chunks(q), chunks(k), chunks(v), chunks(g)
    bcum = jnp.cumsum(gc, axis=2)
    btot = bcum[:, :, -1:]
    k_state = kc * jnp.exp(btot - bcum)
    chunk_decay = jnp.exp(btot[:, :, 0])

    def step(s, inp):
        dec, kst, vv = inp
        s_next = s * dec[..., None] + jnp.einsum("bchk,bchv->bhkv", kst, vv)
        return s_next, s
    s_fin, s_starts = lax.scan(step, s0, (jnp.moveaxis(chunk_decay, 1, 0), jnp.moveaxis(k_state, 1, 0),
                                         jnp.moveaxis(vc, 1, 0)))
    if not emit:
        return None, s_fin
    s_starts = jnp.moveaxis(s_starts, 0, 1)
    q_dec = qc * jnp.exp(bcum)
    k_inv = kc * jnp.exp(-bcum)
    inter = jnp.einsum("bnchk,bnhkv->bnchv", q_dec, s_starts)
    att = jnp.einsum("bnchk,bnshk->bnhcs", q_dec, k_inv)
    att = jnp.where(jnp.tril(jnp.ones((B_CHUNK, B_CHUNK), dtype=bool)), att, 0.0)
    intra = jnp.einsum("bnhcs,bnshv->bnchv", att, vc)
    return (inter + intra).reshape(bsz, t, nh, dv), s_fin

def _merge(f, wkv, o_b, lp):
    bsz, t = wkv.shape[:2]
    mu = jnp.mean(wkv, axis=-1, keepdims=True)
    var = jnp.mean(jnp.square(wkv - mu), axis=-1, keepdims=True)
    y_a = ((wkv - mu) * lax.rsqrt(var + A_LN_EPS)).reshape(bsz, t, A_WIDTH) * lp["a_lnx_g"] + lp["a_lnx_b"]
    bonus = jnp.einsum("bthn,btdhn,hn->bth", f["r"], f["k"], lp["a_r_k"])[..., None] * f["v"]
    y_a = (y_a + bonus.reshape(bsz, t, A_WIDTH)) * jax.nn.silu(f["z_a"])
    ob = o_b * lax.rsqrt(jnp.mean(o_b * o_b, axis=-1, keepdims=True) + EPS) * lp["b_norm_g"]
    y_b = ob.reshape(bsz, t, B_WIDTH) * jax.nn.silu(f["z_b"])
    dt = f["z_a"].dtype
    mixed = (jax.nn.sigmoid(f["g_a"]) * (y_a.astype(dt) @ lp["w_a"])
             + jax.nn.sigmoid(f["g_b"]) * (y_b.astype(dt) @ lp["w_b"]))
    return mixed @ lp["w_out"]

def _mix(f, lp, init, emit):
    sa0, sb0 = init
    a_vec = -f["kk"]
    wkv = 0.0
    s_a = []
    for d, rev in enumerate((False, True)):
        s, y = _rwkv_scan(f["r"], f["decay"][:, :, d], f["k"][:, :, d], f["v"], a_vec,
                          f["kk"] * f["iclr"][:, :, d], sa0[d], rev, emit)
        s_a.append(s)
        if emit:
            wkv = wkv + y
    o_b = 0.0
    s_b = []
    for d in range(2):
        seqs = (f["q"], f["kg"], f["vg"], f["gk"][:, :, d])
        if d == 1:
            seqs = tuple(jnp.flip(z, axis=1) for z in seqs)
        o, s = _gla_chunked(seqs[0], seqs[1], seqs[2], seqs[3], sb0[d], emit)
        s_b.append(s)
        if emit:
            o_b = o_b + (jnp.flip(o, axis=1) if d == 1 else o)
    states = ((s_a[0], s_a[1]), (s_b[0], s_b[1]))
    if not emit:
        return None, states
    return _merge(f, wkv, o_b, lp), states

def first_inputs(seed: int = 0) -> dict:
    key = jax.random.key(seed)
    ks = jax.random.split(key, 26)
    nrm = lambda k, shape, s: jax.random.normal(k, shape, jnp.float32) * s
    L = DEPTH
    conv_id = jnp.zeros((L, 3, 3, 3 * A_WIDTH), jnp.float32).at[:, 1, 1].set(1.0)
    return {
        "x": nrm(ks[0], (BATCH, SEQ, D_MODEL), 1.0),
        "c": nrm(ks[1], (BATCH, D_MODEL), 1.0),
        "ctx": nrm(ks[2], (BATCH, CTX_LEN, D_MODEL), 1.0),
        "c_ctx": nrm(ks[3], (D_MODEL,), 1.0),
        "w_mod": nrm(ks[4], (L, D_MODEL, 3 * D_MODEL), 0.5 * D_MODEL ** -0.5),
        "b_mod": nrm(ks[5], (L, 3 * D_MODEL), 0.01),
        "norm_g": 1.0 + nrm(ks[6], (L, D_MODEL), 0.02),
        "w_in": nrm(ks[7], (L, D_MODEL, P_IN), D_MODEL ** -0.5),
        "conv_w": conv_id + nrm(ks[8], (L, 3, 3, 3 * A_WIDTH), 0.15),
        "a_w0": jax.random.uniform(ks[9], (L, 2, A_WIDTH), jnp.float32, -4.0, 2.0),
        "a_w2": nrm(ks[10], (L, 2, A_DECAY_RANK, A_WIDTH), 0.5 * A_DECAY_RANK ** -0.5),
        "a_a0": nrm(ks[11], (L, 2, A_WIDTH), 0.1),
        "a_a2": nrm(ks[12], (L, 2, A_ICLR_RANK, A_WIDTH), 0.5 * A_ICLR_RANK ** -0.5),
        "a_k_k": 0.85 + nrm(ks[13], (L, A_WIDTH), 0.05),
        "a_k_a": 1.0 + nrm(ks[14], (L, A_WIDTH), 0.05),
        "a_r_k": nrm(ks[15], (L, A_HEADS, A_HEAD), 0.1),
        "a_lnx_g": 1.0 + nrm(ks[16], (L, A_WIDTH), 0.02),
        "a_lnx_b": nrm(ks[17], (L, A_WIDTH), 0.01),
        "b_gk_w2": nrm(ks[18], (L, 2, B_GATE_RANK, B_KEY), B_GATE_RANK ** -0.5),
        "b_gk_b": nrm(ks[19], (L, 2, B_KEY), 0.5),
        "b_norm_g": 1.0 + nrm(ks[20], (L, B_DV), 0.02),
        "w_a": nrm(ks[21], (L, A_WIDTH, D_MODEL), A_WIDTH ** -0.5),
        "w_b": nrm(ks[22], (L, B_WIDTH, D_MODEL), B_WIDTH ** -0.5),
        "w_out": nrm(ks[23], (L, D_MODEL, D_MODEL), D_MODEL ** -0.5),
        "final_g": 1.0 + nrm(ks[24], (D_MODEL,), 0.02),
    }

def first_block(x, c, ctx, c_ctx, w_mod, b_mod, norm_g, w_in, conv_w, a_w0, a_w2, a_a0, a_a2, a_k_k, a_k_a,
              a_r_k, a_lnx_g, a_lnx_b, b_gk_w2, b_gk_b, b_norm_g, w_a, w_b, w_out, final_g):
    bsz = x.shape[0]
    zero_a = jnp.zeros((bsz, A_HEADS, A_HEAD, A_HEAD), jnp.float32)
    zero_b = jnp.zeros((bsz, B_HEADS, B_DK, B_DV), jnp.float32)
    zero_init = ((zero_a, zero_a), (zero_b, zero_b))
    for l in range(DEPTH):
        lp = {"w_in": w_in[l], "conv_w": conv_w[l], "a_w0": a_w0[l], "a_w2": a_w2[l], "a_a0": a_a0[l],
              "a_a2": a_a2[l], "a_k_k": a_k_k[l], "a_k_a": a_k_a[l], "a_r_k": a_r_k[l],
              "a_lnx_g": a_lnx_g[l], "a_lnx_b": a_lnx_b[l], "b_gk_w2": b_gk_w2[l], "b_gk_b": b_gk_b[l],
              "b_norm_g": b_norm_g[l], "w_a": w_a[l], "w_b": w_b[l], "w_out": w_out[l]}
        last = l + 1 == DEPTH
        shift_c, scale_c, gate_c = _modulation(c_ctx, w_mod[l], b_mod[l])
        h_ctx = _rmsnorm(ctx, norm_g[l]) * (1.0 + scale_c) + shift_c
        ctx_out, ctx_states = _mix(_features(h_ctx, lp, grid=False), lp, zero_init, emit=not last)
        shift, scale, gate = _modulation(c, w_mod[l], b_mod[l])
        h = _rmsnorm(x, norm_g[l]) * (1.0 + scale[:, None]) + shift[:, None]
        y, _ = _mix(_features(h, lp, grid=True), lp, ctx_states, emit=True)
        x = x + gate[:, None] * y.astype(x.dtype)
        if not last:
            ctx = ctx + gate_c * ctx_out.astype(ctx.dtype)
    return _rmsnorm(x, final_g)


_first_inputs = first_inputs


def first_inputs(seed=0):
    import zlib

    import numpy as np

    out = dict(_first_inputs(seed))
    spreads = {}
    factors = {}
    for name, (base, spread) in spreads.items():
        noise = np.random.default_rng([zlib.crc32(name.encode()), seed]).standard_normal(out[name].shape)
        drawn = base * np.exp(spread * noise) if base else spread * noise
        out[name] = __import__('jax').numpy.asarray(drawn.astype(out[name].dtype))
    for name, factor in factors.items():
        out[name] = (out[name] * factor).astype(out[name].dtype)
    return out


_narrow_inputs = first_inputs


def first_inputs(seed=0):

    out = dict(_narrow_inputs(seed))
    wider = {'c_ctx': 3.57,
     'b_mod': 6.79,
     'norm_g': 7.49,
     'a_w2': 10.26,
     'a_a0': 9.94,
     'a_k_k': 12.0,
     'a_k_a': 6.85,
     'a_lnx_g': 12.0,
     'a_lnx_b': 12.0,
     'b_gk_w2': 3.47,
     'b_norm_g': 12.0,
     'final_g': 3.19}
    for name, times in wider.items():
        mean = out[name].mean()
        out[name] = (mean + times * (out[name] - mean)).astype(out[name].dtype)
    return out


DEPTH_2 = 2

HEAD_DIM = 128
ROPE_THETA = 10000.0
NORM_EPS = 1e-6
A_HEADS_2 = 8
A_WIDTH_2 = A_HEADS_2 * HEAD_DIM
DIL_CONFIGS = ((128, 1), (512, 4), (2048, 16))
B_VDIM = 2 * HEAD_DIM
B_WIDTH_2 = B_HEADS * B_VDIM
Q_BLOCK = 128
C_HEADS = D_MODEL // HEAD_DIM
C_WIDTH = C_HEADS * HEAD_DIM
MOBA_BLOCK = 256
MOBA_TOPK = 3
MOBA_Q_CHUNK = 16
AB_IN = 3 * A_WIDTH_2 + 3 * B_WIDTH_2 + (A_WIDTH_2 + B_WIDTH_2)
C_IN = 4 * C_WIDTH
N_AB = (DEPTH_2 + 1) // 2
N_C = DEPTH_2 // 2


def _rmsnorm_2(x, g):
    x32 = x.astype(jnp.float32)
    y = x32 * lax.rsqrt(jnp.mean(x32 * x32, axis=-1, keepdims=True) + NORM_EPS)
    return y * g.astype(jnp.float32)

def _rope(t, pos):
    dh = t.shape[-1]
    inv = 1.0 / (ROPE_THETA ** (jnp.arange(0, dh, 2, dtype=jnp.float32) / dh))
    ang = pos.astype(jnp.float32)[:, None] * inv[None, :]
    cos = jnp.concatenate([jnp.cos(ang), jnp.cos(ang)], axis=-1)
    sin = jnp.concatenate([jnp.sin(ang), jnp.sin(ang)], axis=-1)
    x1, x2 = jnp.split(t, 2, axis=-1)
    rot = jnp.concatenate([-x2, x1], axis=-1)
    return t * cos + rot * sin

def _heads(t, n_heads):
    b, s, w = t.shape
    return t.reshape(b, s, n_heads, w // n_heads).transpose(0, 2, 1, 3)

def _merge_2(t):
    b, h, s, d = t.shape
    return t.transpose(0, 2, 1, 3).reshape(b, s, h * d)

def _dilated_group(q, k, v, dil, nback):
    B, H, S, Dh = q.shape
    blk = nback
    L = -(-S // dil)
    L = -(-L // blk) * blk
    Sp = L * dil
    nb = L // blk
    pad = ((0, 0), (0, 0), (0, Sp - S), (0, 0))

    def split(t):
        t = jnp.pad(t, pad).reshape(B, H, L, dil, Dh).transpose(0, 1, 3, 2, 4)
        return t.reshape(B, H, dil, nb, blk, Dh)

    def with_prev(t):
        prev = jnp.pad(t[:, :, :, :-1], ((0, 0), (0, 0), (0, 0), (1, 0), (0, 0), (0, 0)))
        return jnp.concatenate([prev, t], axis=4)

    qs = split(q)
    kk = with_prev(split(k))
    vv = with_prev(split(v))
    s = jnp.einsum('bhrnid,bhrnjd->bhrnij', qs, kk) * (Dh ** -0.5)
    nbi = jnp.arange(nb)[:, None, None]
    i = jnp.arange(blk)[None, :, None]
    j = jnp.arange(2 * blk)[None, None, :]
    rel = blk + i - j
    kidx = (nbi - 1) * blk + j
    mask = (rel >= 0) & (rel <= nback) & (kidx >= 0)
    s = jnp.where(mask, s, -jnp.inf)
    m = jnp.max(s, axis=-1, keepdims=True)
    p = jnp.exp(s - m)
    den = jnp.sum(p, axis=-1, keepdims=True)
    o = jnp.einsum('bhrnij,bhrnjd->bhrnid', p, vv) / den
    lse = m + jnp.log(den)

    def unsplit(t):
        c = t.shape[-1]
        t = t.reshape(B, H, dil, L, c).transpose(0, 1, 3, 2, 4).reshape(B, H, Sp, c)
        return t[:, :, :S]

    return unsplit(o), unsplit(lse)

def _dilated_mixture(q, k, v):
    outs, lses = [], []
    for window, dil in DIL_CONFIGS:
        o, lse = _dilated_group(q, k, v, dil, window // dil)
        outs.append(o)
        lses.append(lse)
    w = jax.nn.softmax(jnp.stack(lses, axis=0), axis=0)
    return jnp.sum(w * jnp.stack(outs, axis=0), axis=0)

def _diff_attention(q1, q2, k1, k2, v, lam):
    B, H, S, Dh = q1.shape
    scale = Dh ** -0.5
    kpos = jnp.arange(S)

    def blk(c):
        start = c * Q_BLOCK
        qa = lax.dynamic_slice_in_dim(q1, start, Q_BLOCK, axis=2)
        qb = lax.dynamic_slice_in_dim(q2, start, Q_BLOCK, axis=2)
        qpos = start + jnp.arange(Q_BLOCK)
        mask = kpos[None, :] <= qpos[:, None]
        p1 = jax.nn.softmax(jnp.where(mask, jnp.einsum('bhid,bhjd->bhij', qa, k1) * scale, -jnp.inf), axis=-1)
        p2 = jax.nn.softmax(jnp.where(mask, jnp.einsum('bhid,bhjd->bhij', qb, k2) * scale, -jnp.inf), axis=-1)
        return jnp.einsum('bhij,bhjd->bhid', p1 - lam * p2, v)

    o = lax.map(blk, jnp.arange(S // Q_BLOCK))
    return o.transpose(1, 2, 0, 3, 4).reshape(B, H, S, v.shape[-1])

def _moba_attention(q, k, v):
    B, H, S, Dh = q.shape
    scale = Dh ** -0.5
    nb = -(-S // MOBA_BLOCK)
    Sp = nb * MOBA_BLOCK
    pad = ((0, 0), (0, 0), (0, Sp - S), (0, 0))
    q, k, v = jnp.pad(q, pad), jnp.pad(k, pad), jnp.pad(v, pad)
    kb = k.reshape(B, H, nb, MOBA_BLOCK, Dh)
    vb = v.reshape(B, H, nb, MOBA_BLOCK, Dh)
    n_sel = min(MOBA_TOPK, nb - 1)
    if n_sel > 0:
        kmean = jnp.mean(kb, axis=3)
        gate = jnp.einsum('bhsd,bhnd->bhsn', q, kmean)
        qblk = jnp.arange(Sp) // MOBA_BLOCK
        past = jnp.arange(nb)[None, :] < qblk[:, None]
        gate = jnp.where(past, gate, -jnp.inf)
        top_vals, top_idx = lax.top_k(gate, n_sel)
        top_valid = jnp.isfinite(top_vals)
    bi = jnp.arange(B)[:, None, None, None]
    hi = jnp.arange(H)[None, :, None, None]

    def step(c):
        start = c * MOBA_Q_CHUNK
        qc = lax.dynamic_slice_in_dim(q, start, MOBA_Q_CHUNK, axis=2)
        b_own = start // MOBA_BLOCK
        ko = lax.dynamic_index_in_dim(kb, b_own, axis=2, keepdims=False)
        vo = lax.dynamic_index_in_dim(vb, b_own, axis=2, keepdims=False)
        qpos = start + jnp.arange(MOBA_Q_CHUNK)
        kpos = b_own * MOBA_BLOCK + jnp.arange(MOBA_BLOCK)
        s_own = jnp.einsum('bhid,bhjd->bhij', qc, ko) * scale
        s_own = jnp.where(kpos[None, :] <= qpos[:, None], s_own, -jnp.inf)
        if n_sel == 0:
            p = jax.nn.softmax(s_own, axis=-1)
            return jnp.einsum('bhij,bhjd->bhid', p, vo)
        ic = lax.dynamic_slice_in_dim(top_idx, start, MOBA_Q_CHUNK, axis=2)
        vc = lax.dynamic_slice_in_dim(top_valid, start, MOBA_Q_CHUNK, axis=2)
        kg = kb[bi, hi, ic]
        vg = vb[bi, hi, ic]
        s_sel = jnp.einsum('bhid,bhikjd->bhikj', qc, kg) * scale
        s_sel = jnp.where(vc[..., None], s_sel, -jnp.inf)
        s_all = jnp.concatenate([s_own, s_sel.reshape(B, H, MOBA_Q_CHUNK, n_sel * MOBA_BLOCK)], axis=-1)
        p = jax.nn.softmax(s_all, axis=-1)
        p_own = p[..., :MOBA_BLOCK]
        p_sel = p[..., MOBA_BLOCK:].reshape(B, H, MOBA_Q_CHUNK, n_sel, MOBA_BLOCK)
        return jnp.einsum('bhij,bhjd->bhid', p_own, vo) + jnp.einsum('bhikj,bhikjd->bhid', p_sel, vg)

    o = lax.map(step, jnp.arange(Sp // MOBA_Q_CHUNK))
    o = o.transpose(1, 2, 0, 3, 4).reshape(B, H, Sp, Dh)
    return o[:, :, :S]

def _layer_ab(x, norm_g, w_in, w_out, lam_vec, subln_g, layer_idx, pos):
    h = jnp.matmul(_rmsnorm_2(x, norm_g).astype(x.dtype), w_in).astype(jnp.float32)
    cuts = np.cumsum([A_WIDTH_2, A_WIDTH_2, A_WIDTH_2, B_WIDTH_2, B_WIDTH_2, B_WIDTH_2]).tolist()
    aq, ak, av, bq, bk, bv, z = jnp.split(h, cuts, axis=-1)
    ya = _dilated_mixture(_rope(_heads(aq, A_HEADS_2), pos), _rope(_heads(ak, A_HEADS_2), pos), _heads(av, A_HEADS_2))
    ya = _merge_2(ya)
    Bn, S = x.shape[0], x.shape[1]
    bq = _rope(bq.reshape(Bn, S, B_HEADS, 2, HEAD_DIM).transpose(0, 2, 3, 1, 4), pos)
    bk = _rope(bk.reshape(Bn, S, B_HEADS, 2, HEAD_DIM).transpose(0, 2, 3, 1, 4), pos)
    bv = _heads(bv, B_HEADS)
    lam_vec = lam_vec.astype(jnp.float32)
    lam_init = 0.8 - 0.6 * math.exp(-0.3 * layer_idx)
    lam = jnp.exp(jnp.sum(lam_vec[0] * lam_vec[1])) - jnp.exp(jnp.sum(lam_vec[2] * lam_vec[3])) + lam_init
    yb = _diff_attention(bq[:, :, 0], bq[:, :, 1], bk[:, :, 0], bk[:, :, 1], bv, lam)
    yb = _rmsnorm_2(yb, subln_g) * (1.0 - lam_init)
    yb = _merge_2(yb)
    y = jnp.concatenate([ya, yb], axis=-1) * jax.nn.silu(z)
    return x + jnp.matmul(y.astype(x.dtype), w_out)

def _layer_c(x, norm_g, w_in, w_out, pos):
    h = jnp.matmul(_rmsnorm_2(x, norm_g).astype(x.dtype), w_in).astype(jnp.float32)
    cq, ck, cv, z = jnp.split(h, [C_WIDTH, 2 * C_WIDTH, 3 * C_WIDTH], axis=-1)
    yc = _moba_attention(_rope(_heads(cq, C_HEADS), pos), _rope(_heads(ck, C_HEADS), pos), _heads(cv, C_HEADS))
    y = _merge_2(yc) * jax.nn.silu(z)
    return x + jnp.matmul(y.astype(x.dtype), w_out)

def second_inputs(seed: int = 0) -> dict:
    key = jax.random.key(seed)
    ks = jax.random.split(key, 10)
    f32 = jnp.float32
    x = jax.random.normal(ks[0], (BATCH, SEQ, D_MODEL), f32)
    norm_ab = 1.0 + 0.02 * jax.random.normal(ks[1], (N_AB, D_MODEL), f32)
    w_in_ab = jax.random.normal(ks[2], (N_AB, D_MODEL, AB_IN), f32) * D_MODEL ** -0.5
    w_out_ab = jax.random.normal(ks[3], (N_AB, A_WIDTH_2 + B_WIDTH_2, D_MODEL), f32) * (A_WIDTH_2 + B_WIDTH_2) ** -0.5
    lam_ab = 0.1 * jax.random.normal(ks[4], (N_AB, 4, HEAD_DIM), f32)
    subln_ab = 1.0 + 0.02 * jax.random.normal(ks[5], (N_AB, B_VDIM), f32)
    norm_c = 1.0 + 0.02 * jax.random.normal(ks[6], (N_C, D_MODEL), f32)
    w_in_c = jax.random.normal(ks[7], (N_C, D_MODEL, C_IN), f32) * D_MODEL ** -0.5
    w_out_c = jax.random.normal(ks[8], (N_C, C_WIDTH, D_MODEL), f32) * C_WIDTH ** -0.5
    final_norm = 1.0 + 0.02 * jax.random.normal(ks[9], (D_MODEL,), f32)
    return {"x": x, "norm_ab": norm_ab, "w_in_ab": w_in_ab, "w_out_ab": w_out_ab,
            "lam_ab": lam_ab, "subln_ab": subln_ab, "norm_c": norm_c, "w_in_c": w_in_c,
            "w_out_c": w_out_c, "final_norm": final_norm}

def second_block(x, norm_ab, w_in_ab, w_out_ab, lam_ab, subln_ab, norm_c, w_in_c, w_out_c, final_norm):
    pos = jnp.arange(x.shape[1], dtype=jnp.int32)
    h = x
    for i in range(DEPTH_2):
        j = i // 2
        if i % 2 == 0:
            h = _layer_ab(h, norm_ab[j], w_in_ab[j], w_out_ab[j], lam_ab[j], subln_ab[j], i, pos)
        else:
            h = _layer_c(h, norm_c[j], w_in_c[j], w_out_c[j], pos)
    return _rmsnorm_2(h, final_norm).astype(x.dtype)


def setup_inputs(seed=0):
    out = dict(first_inputs(seed))
    for name, value in second_inputs(seed + 1).items():
        if name != "x":
            out[name + "_2"] = value
    return out


def reference(
    x, c, ctx, c_ctx, w_mod, b_mod, norm_g, w_in, conv_w, a_w0, a_w2, a_a0, a_a2, a_k_k, a_k_a,
    a_r_k, a_lnx_g, a_lnx_b, b_gk_w2, b_gk_b, b_norm_g, w_a, w_b, w_out, final_g, norm_ab_2,
    w_in_ab_2, w_out_ab_2, lam_ab_2, subln_ab_2, norm_c_2, w_in_c_2, w_out_c_2, final_norm_2,
):
    x = first_block(
        x, c, ctx, c_ctx, w_mod, b_mod, norm_g, w_in, conv_w, a_w0, a_w2, a_a0, a_a2, a_k_k,
        a_k_a, a_r_k, a_lnx_g, a_lnx_b, b_gk_w2, b_gk_b, b_norm_g, w_a, w_b, w_out, final_g,
    )
    return second_block(
        x, norm_ab_2, w_in_ab_2, w_out_ab_2, lam_ab_2, subln_ab_2, norm_c_2, w_in_c_2,
        w_out_c_2, final_norm_2,
    )


_drawn_inputs = setup_inputs


def setup_inputs(seed=0):
    import zlib

    import numpy as np

    out = dict(_drawn_inputs(seed))
    spreads = {}
    factors = {'norm_ab_2': 4.393, 'subln_ab_2': 8.0, 'norm_c_2': 8.0, 'final_norm_2': 2.84}
    for name, (base, spread) in spreads.items():
        noise = np.random.default_rng([zlib.crc32(name.encode()), seed]).standard_normal(out[name].shape)
        drawn = base * np.exp(spread * noise) if base else spread * noise
        out[name] = __import__('jax').numpy.asarray(drawn.astype(out[name].dtype))
    for name, factor in factors.items():
        out[name] = (out[name] * factor).astype(out[name].dtype)
    return out
```

```python
import math
from contextlib import ExitStack

import concourse.bass as bass
from concourse import mybir

F32 = mybir.dt.float32
F32R = mybir.dt.float32r
ALU = mybir.AluOpType
ACT = mybir.ActivationFunctionType
AX = mybir.AxisListType

P = 128
T = 256
KT = 16
UK = 8
RING = 4
LEAD = 3
C = 64
EPS = 1e-6
LN_EPS = 64e-5
PAIRS = 8
GH = 4
DECAY = math.exp(-0.5)

WORK = 19100
U_MOD = 96
U_LORA, U_PAIR, U_GLA, U_MERGE, U_OUT, U_HEAD, U_DIFF = 6, 8, 12, 6, 2, 8, 16
S_LORA = 0
S_PAIR = S_LORA + U_LORA
S_GLA = S_PAIR + U_PAIR * PAIRS
S_MERGE = S_GLA + U_GLA * GH
S_OUT1 = S_MERGE + U_MERGE * KT
S_DIL = S_OUT1 + U_OUT * KT
S_DIFF = S_DIL + U_HEAD * 8
S_OUT2 = S_DIFF + U_DIFF * 4
S_CAUS = S_OUT2 + U_OUT * KT
S_OUT3 = S_CAUS + U_HEAD * 16
S_END = S_OUT3 + U_OUT * KT

PV = {}
_n = 0
for _name, _w in (("norm_g", KT), ("b_mod", 48), ("final_g", KT), ("norm_ab", KT), ("norm_c", KT),
                  ("final_norm", KT), ("b_norm_g", 2), ("subln", 2), ("gk_b", 8), ("lam", 4), ("cond", 32)):
    PV[_name] = slice(_n, _n + _w)
    _n += _w
NPV = _n
PP = {"k": 0, "v": 9, "r": 18, "w0": 27, "a0": 29, "k_k": 31, "k_a": 32, "r_k": 33, "ln_g": 34, "ln_b": 35}
PP_W2, PP_A2, NPP = 36, 36 + P, 36 + 2 * P
CN = {}
_n = 0
for _name, _w in (("ident", P), ("mean", P), ("head", P), ("keep", 2 * 512), ("strict", 2 * C), ("incl", 2 * C),
                  ("level", 6 * 2 * P), ("gmask", 2 * P)):
    CN[_name] = slice(_n, _n + _w)
    _n += _w
NCN = _n
CN2 = {"cos": slice(0, 512), "sin": slice(512, 1024), "dil": slice(1024, 1024 + 384), "caus": slice(1408, 1408 + 384)}
NCN2 = 1408 + 384


def build(nc, stream, xT, par, pair_par, gk_w, consts, consts2, outT):
    ctx = ExitStack()
    with ctx:
        def sb(name, cols, dt=F32, parts=P):
            return ctx.enter_context(nc.sbuf_tensor(name, [parts, cols], dt))

        def sem(name):
            return ctx.enter_context(nc.semaphore(name))

        raw = [sb(f"raw{r}", UK * P).ap().rearrange("p (k n) -> p k n", k=UK) for r in range(RING)]
        whi = [sb(f"whi{r}", UK * P, F32R).ap().rearrange("p (k n) -> p k n", k=UK) for r in range(RING)]
        wlo = [sb(f"wlo{r}", UK * P, F32R).ap().rearrange("p (k n) -> p k n", k=UK) for r in range(RING)]
        ahi = sb("ahi", 2 * KT * T, F32R).ap().rearrange("p (s k t) -> p s k t", s=2, k=KT)
        alo = sb("alo", 2 * KT * T, F32R).ap().rearrange("p (s k t) -> p s k t", s=2, k=KT)
        cns = sb("cns", NCN)
        pv = sb("pv", NPV)
        ident = cns[:, CN["ident"]]
        meanw = cns[:, CN["mean"]]
        headw = cns[:, CN["head"]]
        small = sb("small", 128)
        mod = sb("mod", 96)
        gmul = sb("gmul", 2 * KT)
        ps = ctx.enter_context(nc.psum_tensor("ps", [P, 8, 512], F32))

        free, fresh = [], []

        class Count:

            def __init__(self, handle, base, per, trips):
                self.sem, self.base, self.end = handle, base, base + per * trips

            def wait(self, eng, value):
                eng.wait_ge(self.sem, value + self.base)

        def counts(phase, spec, trips):
            out = {}
            for word in spec.split():
                name, _, per = word.partition(":")
                if free:
                    handle, base = free.pop(0)
                else:
                    handle, base = sem(f"{phase}_{name}"), 1
                    fresh.append(handle)
                if "=" in name:
                    name, per = name.split("=")
                    out[name] = Count(handle, base, int(per), 1)
                else:
                    out[name] = Count(handle, base, int(per or 1), trips)
            return out

        def open_counts(sp):
            for handle in fresh:
                sp.sem_inc(handle, 1)

        def retire(old):
            free.extend((c.sem, c.end) for c in old.values())

        raw_in = [sem(f"raw_in{r}") for r in range(RING)]
        mod_used = sem("mod_used")
        hi_done = sem("hi_done")
        lo_done = sem("lo_done")
        unit_used = sem("unit_used")

        def chain(name):
            s = sem(name)
            count = [0]

            def link(eng, ins):
                count[0] += 1
                ins.then_inc(s, 1)
                eng.wait_ge(s, count[0])
            link.sem, link.count = s, count
            return link

        def load_unit(sp, slot, unit):
            sp.dma_start(raw[slot].rearrange("p k n -> p (k n)"), stream[bass.ds(unit, 1)].rearrange("a p n -> (a p) n")
                         if not isinstance(unit, int) else stream[unit]).then_inc(raw_in[slot], 16)

        def split_hi(act, slot, s):
            if isinstance(s, int):
                rounds = (U_MOD + s) // RING + 1
            else:
                i, per, k = s
                rounds = i * (per // RING) + (U_MOD + k) // RING + 1
                s = i * per + k
            act.wait_ge(raw_in[slot], rounds * 16)
            if not isinstance(s, int) or s >= RING:
                act.wait_ge(unit_used, s - (RING - 1))
            nc.scalar.activation(whi[slot], raw[slot], ACT.Copy).then_inc(hi_done, 1)

        def split_lo(pool, slot, s):
            if not isinstance(s, int):
                i, per, k = s
                s = i * per + k
            pool.wait_ge(hi_done, s + 1)
            if not isinstance(s, int) or s >= RING:
                pool.wait_ge(unit_used, s - (RING - 1))
            nc.gpsimd.tensor_tensor(wlo[slot], raw[slot], whi[slot].bitcast(F32), ALU.subtract).then_inc(lo_done, 1)

        def mm_unit(pe, slot, s, out, sel, k0, first, last, hi_=None, lo_=None, tile_ready=None):
            pe.wait_ge(lo_done, s + 1)
            ins = None
            for k in range(UK):
                if tile_ready is not None:
                    tile_ready(k0 + k)
                mh, ml = (ahi[:, sel, k0 + k, :], alo[:, sel, k0 + k, :]) if hi_ is None else \
                    (hi_[:, k0 + k, :], lo_[:, k0 + k, :])
                nc.tensor.matmul(out, whi[slot][:, k, :], mh, start=first and k == 0, stop=False)
                nc.tensor.matmul(out, whi[slot][:, k, :], ml, start=False, stop=False)
                ins = nc.tensor.matmul(out, wlo[slot][:, k, :], mh, start=False, stop=last and k == UK - 1)
            return ins.then_inc(unit_used, 1)

        def mm_tile(pe, base, i, per, k, out, sel, tile_ready=None):
            mm_unit(pe, (base + k) % RING, i * per + (base + k), out, sel, 0, True, False, tile_ready=tile_ready)
            return mm_unit(pe, (base + k + 1) % RING, i * per + (base + k + 1), out, sel, UK, False, True,
                           tile_ready=tile_ready)

        both = slice(0, 2)

        work_stack = ctx.enter_context(ExitStack())
        LWA = work_stack.enter_context(nc.sbuf_tensor("LWA", [P, 2, 512], F32))
        LG = work_stack.enter_context(nc.sbuf_tensor("LG", [32, 512], F32))
        W = work_stack.enter_context(nc.sbuf_tensor("W", [P, WORK], F32))
        xin = W[:, 0:2 * KT * T].rearrange("p (s k t) -> p s k t", s=2, k=KT)
        sq = W[:, 8192:8192 + 1024].rearrange("p (b s t) -> p b s t", b=2, s=2)
        rstd = W[:, 9216:9728]
        hf = W[:, 9728:9728 + 2048].rearrange("p (b s t) -> p b s t", b=4, s=2)

        modrow = W[0:2, 11776:11776 + 48 * P]

        s_par = sem("s_par")
        s_x = sem("s_x")
        s_silu = sem("s_silu")
        s_sq = sem("s_sq")
        s_sqmm = sem("s_sqmm")
        s_ms = sem("s_ms")
        s_root = sem("s_root")
        s_rstd = sem("s_rstd")
        s_xn = sem("s_xn")
        s_modmm = sem("s_modmm")
        modcp = counts("mod", "rows:2", U_MOD // 8)["rows"]
        s_mod = sem("s_mod")
        s_h = sem("s_h")
        s_hhi = sem("s_hhi")
        s_hlo = sem("s_hlo")
        s_pre = sem("s_pre")
        s_dve0 = chain("s_dve0")
        cond = pv[:, PV["cond"]].rearrange("p (k c) -> p k c", c=2)
        scond = small[:, 0:32].rearrange("p (k c) -> p k c", c=2)
        mod_v = mod[:, :].rearrange("p (n c) -> p n c", c=2)
        gm_v = gmul[:, :].rearrange("p (n c) -> p n c", c=2)

        def sp_start(sp):
            sp.dma_start(pv[:, :], par).then_inc(s_par, 16)
            sp.dma_start(cns[:, :], consts).then_inc(s_par, 16)
            for u in range(RING):
                load_unit(sp, u, u)
            sp.dma_start(xin, xT).then_inc(s_x, 16)

        def sp_mod(sp):
            with sp.Fori(1, U_MOD // RING) as i:
                for r in range(RING):
                    sp.wait_ge(mod_used, i * RING + (r - RING + 1))
                    load_unit(sp, r, i * RING + r)

        def sp_stream(sp):
            for s in range(U_LORA):
                if s < RING:
                    sp.wait_ge(mod_used, U_MOD + s - RING + 1)
                else:
                    sp.wait_ge(lo_done, s - RING + 1)
                load_unit(sp, s % RING, U_MOD + s)

        def sp_loop(sp, base, n):
            with sp.Fori(0, n // RING) as i:
                for r in range(RING):
                    sp.wait_ge(lo_done, i * RING + (base + r - RING + 1))
                    load_unit(sp, (base + r) % RING, i * RING + (U_MOD + base + r))

        def act_start(act):
            act.wait_ge(s_par, 32)
            nc.scalar.activation(small[:, 32:64], pv[:, PV["cond"]], ACT.Tanh, scale=0.5).then_inc(s_silu, 1)
            act.wait_ge(s_x, 16)
            for k in range(KT):
                if k >= 2:
                    act.wait_ge(s_sqmm, k - 1)
                nc.scalar.activation(sq[:, k % 2], xin[:, :, k, :], ACT.Square).then_inc(s_sq, 1)
            act.wait_ge(s_ms, 1)
            nc.scalar.activation(rstd, rstd, ACT.Sqrt).then_inc(s_root, 1)

        def dve_start(dve):
            dve.wait_ge(s_silu, 1)
            s_dve0(dve, nc.vector.scalar_tensor_tensor(small[:, 32:64], small[:, 32:64], 1.0, pv[:, PV["cond"]],
                                                       ALU.add, ALU.mult))
            nc.vector.tensor_scalar(small[:, 0:32], small[:, 32:64], 0.5, None, ALU.mult).then_inc(s_pre, 1)

        def dve_norm(dve):
            dve.wait_ge(s_sqmm, KT)
            nc.vector.tensor_scalar(rstd, ps[:, 7, :], EPS, None, ALU.add).then_inc(s_ms, 1)
            dve.wait_ge(s_root, 1)
            nc.vector.reciprocal(rstd, rstd).then_inc(s_rstd, 1)
            dve.wait_ge(s_rstd, 1)
            r3 = rstd.rearrange("p (s t) -> p s t", s=2)
            for k in range(KT):
                nc.vector.tensor_tensor(xin[:, :, k, :], xin[:, :, k, :], r3, ALU.mult).then_inc(s_xn, 1)

        def pe_norm(pe):
            for k in range(KT):
                pe.wait_ge(s_sq, k + 1)
                nc.tensor.matmul(ps[:, 7, :], meanw, sq[:, k % 2], start=k == 0, stop=k == KT - 1).then_inc(s_sqmm, 1)

        def mod_rounds(pe, first, end):
            with pe.Fori(first, end) as i:
                for g in range(2):
                    if g == 0:
                        modcp.wait(pe, i * 2)
                    for t in range(2):
                        for u in range(2):
                            r = 2 * t + u
                            pe.wait_ge(raw_in[r], (i * 2 + g) * 16 + 16)
                            for k in range(UK):
                                ins = nc.tensor.matmul(ps[0:2, g, t * P:(t + 1) * P], scond[:, UK * u + k, :],
                                                       raw[r][:, k, :], start=u == 0 and k == 0,
                                                       stop=u == 1 and k == UK - 1)
                            ins.then_inc(mod_used, 1)

        def pe_mod(pe):
            pe.wait_ge(s_pre, 1)
            mod_rounds(pe, 0, U_MOD // 16)
            pe_norm(pe)
            mod_rounds(pe, U_MOD // 16, U_MOD // 8)
            for n in range(48):
                modcp.wait(pe, n // 2 + 1)
                nc.tensor.transpose(ps[:, 2, 2 * n:2 * n + 2], modrow[:, n * P:(n + 1) * P],
                                    ident[0:2, 0:2]).then_inc(s_modmm, 1)

        def dve_rows(dve, first, end):
            with dve.Fori(first, end) as i:
                for g in range(2):
                    dve.wait_ge(mod_used, i * 8 + 4 * g + 4)
                    nc.vector.tensor_copy(modrow[:, bass.ds((i * 2 + g) * 2 * P, 2 * P)],
                                          ps[0:2, g, 0:2 * P]).then_inc(modcp.sem, 1)

        def dve_mod(dve):
            dve_rows(dve, 0, U_MOD // 16)
            dve_norm(dve)
            dve_rows(dve, U_MOD // 16, U_MOD // 8)
            dve.wait_ge(s_modmm, 48)
            bias = pv[:, PV["b_mod"]].unsqueeze(2).broadcast_to([P, 48, 2])
            rows = ps[:, 2, 0:96].rearrange("p (n c) -> p n c", c=2)
            nc.vector.tensor_tensor(mod_v, rows, bias, ALU.add).then_inc(s_mod, 1)
            dve.wait_ge(s_mod, 1)
            g = pv[:, PV["norm_g"]].unsqueeze(2).broadcast_to([P, KT, 2])
            nc.vector.scalar_tensor_tensor(gm_v, mod_v[:, KT:2 * KT, :], 1.0, g, ALU.add, ALU.mult).then_inc(s_mod, 1)
            dve.wait_ge(s_mod, 2)
            dve.wait_ge(s_xn, KT)
            for k in range(KT):
                if k >= 4:
                    dve.wait_ge(s_hlo, k - 3)
                for s in range(2):
                    nc.vector.tensor_scalar(hf[:, k % 4, s], xin[:, s, k, :], gm_v[:, k, s:s + 1], mod_v[:, k, s:s + 1],
                                            ALU.mult, ALU.add).then_inc(s_h, 1)

        def act_h(act):
            for s in range(RING):
                split_hi(act, s, s)
            for k in range(KT):
                act.wait_ge(s_h, 2 * k + 2)
                nc.scalar.activation(ahi[:, :, k, :], hf[:, k % 4], ACT.Copy).then_inc(s_hhi, 1)

        def pool_h(pool):
            for s in range(RING):
                split_lo(pool, s, s)
            for k in range(KT):
                pool.wait_ge(s_h, 2 * k + 2)
                pool.wait_ge(s_hhi, k + 1)
                nc.gpsimd.tensor_tensor(alo[:, :, k, :], hf[:, k % 4], ahi[:, :, k, :].bitcast(F32),
                                        ALU.subtract).then_inc(s_hlo, 1)

        s_lora = sem("s_lora")
        s_lcp = sem("s_lcp")

        def pe_lora(pe):
            for t in range(3):
                mm_tile(pe, S_LORA, 0, 0, 2 * t, ps[:, 2 + t, :], both,
                        tile_ready=(lambda k: pe.wait_ge(s_hlo, k + 1)) if t == 0 else None)

        def act_lora(act):
            for s in range(RING, U_LORA + LEAD):
                split_hi(act, s % RING, s)
            act.wait_ge(unit_used, 2)
            nc.scalar.activation(LWA[:, 0, :], ps[:, 2, :], ACT.Tanh).then_inc(s_lcp, 1)
            act.wait_ge(unit_used, 4)
            nc.scalar.activation(LWA[:, 1, :], ps[:, 3, :], ACT.Copy).then_inc(s_lcp, 1)
            act.wait_ge(unit_used, 6)
            nc.scalar.activation(LG[:, :], ps[0:32, 4, :], ACT.Copy).then_inc(s_lcp, 1)

        def pool_lora(pool):
            for s in range(RING, U_LORA + LEAD):
                split_lo(pool, s % RING, s)

        place = [0]

        def area(cols):
            a = place[0]
            place[0] += cols
            assert place[0] <= WORK, place[0]
            return W[:, a:a + cols]

        YA = area(KT // 2 * T).rearrange("p (k t) -> p k t", t=T)
        dd = "p (d t) -> p d t"
        AR = area(2048).rearrange("p (d a t) -> p d a t", d=2, a=2)
        KA = area(1024).rearrange(dd, d=2)
        BE = area(1024).rearrange(dd, d=2)
        PD = area(1024).rearrange(dd, d=2)
        TW = area(1024).rearrange(dd, d=2)
        CW = area(1024).rearrange(dd, d=2)
        TA = area(1024).rearrange(dd, d=2)
        hdc = "p (h d c t) -> p h d c t"
        MB = area(1024).rearrange(hdc, h=2, d=2, c=4)
        MK = area(1024).rearrange(hdc, h=2, d=2, c=4)
        BKR = area(1024)
        BKR5 = BKR.rearrange("p (h b d c t) -> p h b d c t", h=2, b=2, d=2, c=2)
        WV = MB.rearrange("p h d c t -> p (h d c t)").rearrange("p (d c f) -> p d c f", d=2, c=4)
        tok1 = area(1024)
        tok2 = area(1024)
        BT = tok1.rearrange("p (d c f) -> p d c f", d=2, c=4)
        KTK = tok2.rearrange("p (d c f) -> p d c f", d=2, c=4)
        kkn, ksq, kc = tok1[:, 0:512], tok1[:, 512:1024], tok2[:, 0:512]
        VT = area(512).rearrange("p (c f) -> p c f", c=4)
        vc = area(512)
        bon = area(256)
        padx = [area(396).rearrange("p (y x) -> p y x", y=6) for _ in range(2)]
        padc = [area(258) for _ in range(2)]
        rc, zs = AR[:, 0, 1, T:], AR[:, 1, 1, T:]
        ST = area(256).rearrange("p (b d v) -> p b d v", b=2, d=2)
        SP_ = area(128).rearrange("p (d v) -> p d v", d=2)
        UU, RR = CW[:, 0, 0:P], CW[:, 0, P:2 * P]
        pst = area(NPP)
        pp = area(NPP)
        hpar = area(8)
        X, XT, MKL, YY = (v.rearrange("p d (c t) -> p d c t", c=4) for v in (TA, KA, TW, CW))
        XTF = BE.rearrange("p h (d c t) -> p h d c t", d=2, c=4)
        parts = (slice(0, C), slice(C, P))
        ysum, ydev = TW[:, 0, 0:T], TW[:, 0, T:]
        ytmp, yrs = TW[:, 1, 0:T], TW[:, 1, T:]
        kst_ = small[:, 64:68]
        level = cns[:, CN["level"]].rearrange("p (l d b t) -> p l d b t", l=6, d=2, b=2)
        strict = cns[:, CN["strict"]].rearrange("p (d t) -> p d t", d=2)
        incl = cns[:, CN["incl"]].rearrange("p (d t) -> p d t", d=2)
        keep = cns[:, CN["keep"]].rearrange("p (d t) -> p d t", d=2)
        ORDER = ((4, 5, 6, 7, 0, 1, 2, 3), (7, 6, 5, 4, 3, 2, 1, 0))

        names = ("pst_in:16 pst_free:1 hp:1 pad_k:2 pad_v:2 pad_r:1 conv_k:12 conv_v:12 conv_r:9 kk:1 kksq:1 "
                 "nrm_mm:1 lnn:1 rsn:1 kkn_ok:1 lora_mm:4 tw_ok:2 ta_ok:2 logw:1 cw:2 cwm:1 exps:3 ar_ok:1 "
                 "be1:1 be_ok:1 kd:1 kd2:1 ka_ok:1 rho_ok:1 bon1:1 bon_ok:1 z_ok:1 tz:1 bonus_mm:1 prod_q:1 "
                 "prod_b:1 prod_a:1 prod_k:1 ev_mb:2 ev_q:2 wv_mm:1 wv_ok:1 y0a:1 y0b:1 ev_x1:4 ev_x:4 "
                 "ev_xt1:4 ev_xt:4 ev_mk:2 vt_mm:1 bt_mm:1 kt_mm:1 vt_ok:1 bt_ok:1 kt_ok:1 lvl_m:20 y_lvl:20 "
                 "xtf:8 y_ev:20 xa_mm:16 xta_mm:20 x_up:16 xt_up:16 rhs_mm:14 rhs_ev:16 u_mm:16 u_ev:16 ds_mm:14 "
                 "sp_ok:12 st_ok:14 yo_mm:4 y0_mm:1 y0_ok:1 ys_ok:1 mean_mm:1 dev_ok:1 dsq:1 var_mm:1 lnv:1 rsv:1 "
                 "y1:1 y2:1 y3:1 y4:1 pair_done:1 kconst=19 pad_zero=4")
        R = counts("r", names, PAIRS)

        def sp_pairs(sp):
            with sp.Fori(0, PAIRS) as i:
                R["pst_free"].wait(sp, i)
                sp.dma_start(pst, pair_par[bass.ds(i, 1)].rearrange("a p n -> (a p) n")).then_inc(R["pst_in"].sem, 16)
                for r in range(U_PAIR):
                    sp.wait_ge(lo_done, i * U_PAIR + (S_PAIR + r - RING + 1))
                    load_unit(sp, (S_PAIR + r) % RING, i * U_PAIR + (U_MOD + S_PAIR + r))

        def pe_chunks(h, d, c):
            return slice(C * h, C * h + C), slice(C * (c % 2), C * (c % 2) + C), c // 2, slice(C * c, C * c + C)

        passed = sem("passed")

        def apart(pe):
            pe.sem_inc(passed, 1)

        def pe_pairs(pe):
            with pe.Fori(0, PAIRS) as i:
                base = S_PAIR
                R["kkn_ok"].wait(pe, i)
                mm_tile(pe, base, i, U_PAIR, 0, ps[:, 0, :], both)
                R["pair_done"].wait(pe, i)
                R["hp"].wait(pe, i + 1)
                for d in range(2):
                    q = slice(64 * d, 64 * d + 64)
                    for a in range(2):
                        nc.tensor.matmul(ps[:, 4 + 2 * a + d, :], pp[q, PP_W2 + P * a:PP_W2 + P * a + P],
                                         LWA[q, a, :], start=True, stop=True).then_inc(R["lora_mm"].sem, 1)
                mm_tile(pe, base, i, U_PAIR, 2, ps[:, 2, 0:T], 0)
                mm_unit(pe, (base + 4) % RING, i * U_PAIR + (base + 4), ps[:, 1, :], both, 0, True, False)
                R["kksq"].wait(pe, i + 1)
                nc.tensor.matmul(ps[:, 0, :], headw, ksq, start=True, stop=True).then_inc(R["nrm_mm"].sem, 1)
                mm_unit(pe, (base + 5) % RING, i * U_PAIR + (base + 5), ps[:, 1, :], both, UK, False, True)
                mm_tile(pe, base, i, U_PAIR, 6, ps[:, 3, 0:T], 0)

                def square(bank, left, right, done):
                    for d in range(2):
                        for c in range(8):
                            for h in range(2):
                                f, tk, tile, cols = pe_chunks(h, d, c)
                                o = (d * 4 + tile) * C
                                ins = nc.tensor.matmul(ps[tk, bank + h, o:o + C], left[f, d, cols], right[f, d, cols],
                                                       start=True, stop=True)
                    ins.then_inc(R[done].sem, 1)

                alpha = AR[:, :, 0, :]
                R["be_ok"].wait(pe, i + 1)
                apart(pe)
                square(4, BE, alpha, "prod_b")
                R["z_ok"].wait(pe, i + 1)
                apart(pe)
                square(2, alpha, BE, "prod_a")
                R["ka_ok"].wait(pe, i + 1)
                R["pad_v"].wait(pe, 2 * i + 2)
                apart(pe)
                square(0, KA, alpha, "prod_k")
                R["ev_mb"].wait(pe, 2 * i + 2)
                for d in range(2):
                    for t in range(4):
                        ins = nc.tensor.transpose(ps[:, 4 + d, P * t:P * t + P], BE[:, d, P * t:P * t + P], ident)
                ins.then_inc(R["bt_mm"].sem, 1)
                R["rho_ok"].wait(pe, i + 1)
                apart(pe)
                for b, vec in enumerate((BE, KA)):
                    for d in range(2):
                        for c in range(4):
                            for h in range(2):
                                f, tk, tile, cols = pe_chunks(h, d, c)
                                o = ((b * 2 + d) * 2 + tile) * C
                                ins = nc.tensor.matmul(ps[tk, 6 + h, o:o + C], vec[f, d, cols], AR[f, d, 1, cols],
                                                       start=True, stop=True)
                ins.then_inc(R["prod_q"].sem, 1)
                R["ev_mk"].wait(pe, 2 * i + 2)
                for t in range(4):
                    ins = nc.tensor.transpose(ps[:, 2, P * t:P * t + P], vc[:, P * t:P * t + P], ident)
                ins.then_inc(R["vt_mm"].sem, 1)
                for d in range(2):
                    for t in range(4):
                        ins = nc.tensor.transpose(ps[:, d, P * t:P * t + P], KA[:, d, P * t:P * t + P], ident)
                ins.then_inc(R["kt_mm"].sem, 1)
                R["bt_ok"].wait(pe, i + 1)
                R["kt_ok"].wait(pe, i + 1)
                R["ev_q"].wait(pe, 2 * i + 2)

                def blocks(d, bank, left, right, done):
                    for c in range(4):
                        ins = nc.tensor.matmul(ps[:, bank + d, P * c:P * c + P], left[:, d, c], right[:, d, c],
                                               start=True, stop=True)
                    ins.then_inc(R[done].sem, 1)

                for h in range(2):
                    for lv in range(5):
                        for d in range(2):
                            R["lvl_m"].wait(pe, i * 20 + h * 10 + lv * 2 + d + 1)
                            if lv == 0:
                                R["ev_x"].wait(pe, i * 4 + 2 * h + d + 1)
                            else:
                                R["x_up"].wait(pe, i * 16 + h * 8 + (lv - 1) * 2 + d + 1)
                            blocks(d, 4, MKL, X, "y_lvl")
                        for d in range(2):
                            R["y_ev"].wait(pe, i * 20 + h * 10 + lv * 2 + d + 1)
                            if lv == 0:
                                R["ev_xt"].wait(pe, i * 4 + 2 * h + d + 1)
                            else:
                                R["xt_up"].wait(pe, i * 16 + h * 8 + (lv - 1) * 2 + d + 1)
                            if lv < 4:
                                blocks(d, 6, XT, YY, "xa_mm")
                            blocks(d, 0, YY, XT, "xta_mm")
                R["xtf"].wait(pe, i * 8 + 8)
                R["vt_ok"].wait(pe, i + 1)
                apart(pe)
                for d in range(2):
                    for c in range(8):
                        for h in range(2):
                            f, tk, tile, cols = pe_chunks(h, d, c)
                            o = tile * P + C * h
                            ins = nc.tensor.matmul(ps[tk, d, o:o + C], MK[tk, h, d, tile], VT[tk, tile, C * h:C * h + C],
                                                   start=True, stop=True)
                ins.then_inc(R["wv_mm"].sem, 1)
                R["wv_ok"].wait(pe, i + 1)
                apart(pe)

                def step(d, q):
                    for h in range(2):
                        yield pe_chunks(h, d, ORDER[d][q]) + (h, slice(C * h, C * h + C))

                for q in range(8):
                    if q:
                        for d in range(2):
                            R["st_ok"].wait(pe, i * 14 + 2 * (q - 1) + d + 1)
                            apart(pe)
                            for f, tk, tile, cols, h, o in step(d, q):
                                ins = nc.tensor.matmul(ps[tk, 4 + h, 0:C], AR[f, d, 0, cols], ST[f, q % 2, d],
                                                       start=True, stop=True)
                            ins.then_inc(R["rhs_mm"].sem, 1)
                    if q < 7:
                        for d in range(2):
                            for f, tk, tile, cols, h, o in step(d, q):
                                nc.tensor.matmul(ps[f, 2 + d, 0:C], KTK[tk, d, tile, o], VT[tk, tile, o], start=True,
                                                 stop=False)
                    for d in range(2):
                        R["rhs_ev"].wait(pe, i * 16 + 2 * q + d + 1)
                        apart(pe)
                        for f, tk, tile, cols, h, o in step(d, q):
                            ins = nc.tensor.matmul(ps[tk, 6, o], XTF[tk, h, d, tile], RR[tk, o], start=True, stop=True)
                        ins.then_inc(R["u_mm"].sem, 1)
                    if q >= 4:
                        for d in range(2):
                            for f, tk, tile, cols, h, o in step(d, q):
                                ins = nc.tensor.matmul(ps[f, 7, d * T + cols.start:d * T + cols.stop], ST[f, q % 2, d],
                                                       AR[f, d, 1, cols], start=True, stop=True)
                        if q == 7:
                            ins.then_inc(R["y0_mm"].sem, 1)
                    for d in range(2):
                        R["u_ev"].wait(pe, i * 16 + 2 * q + d + 1)
                        apart(pe)
                        if q < 7:
                            for f, tk, tile, cols, h, o in step(d, q):
                                ins = nc.tensor.matmul(ps[f, 2 + d, 0:C], BT[tk, d, tile, o], UU[tk, o], start=False,
                                                       stop=True)
                            ins.then_inc(R["ds_mm"].sem, 1)
                    if q >= 4:
                        for d in range(2):
                            for f, tk, tile, cols, h, o in step(d, q):
                                nc.tensor.matmul(ps[f, d, cols], UU[tk, o], BKR5[tk, h, 0, d, tile], start=True, stop=False)
                                ins = nc.tensor.matmul(ps[f, d, cols], VT[tk, tile, o], BKR5[tk, h, 1, d, tile],
                                                       start=False, stop=True)
                        ins.then_inc(R["yo_mm"].sem, 1)
                R["bon_ok"].wait(pe, i + 1)
                nc.tensor.matmul(ps[:, 6, 0:T], headw, bon, start=True, stop=True).then_inc(R["bonus_mm"].sem, 1)
                R["ys_ok"].wait(pe, i + 1)
                nc.tensor.matmul(ps[:, 4, 0:T], headw, ysum, start=True, stop=True).then_inc(R["mean_mm"].sem, 1)
                R["dsq"].wait(pe, i + 1)
                nc.tensor.matmul(ps[:, 5, 0:T], headw, ytmp, start=True, stop=True).then_inc(R["var_mm"].sem, 1)

        def act_pairs(act):
            R["pad_zero"].wait(act, 4)
            with act.Fori(0, PAIRS) as i:
                def hi(k):
                    split_hi(act, (S_PAIR + k + LEAD) % RING, (i, U_PAIR, S_PAIR + k + LEAD))

                def to_pad(bank, b, name, with_ctx, free, n):
                    act.wait_ge(unit_used, i * U_PAIR + (S_PAIR + n))
                    R[free[0]].wait(act, free[1])
                    nc.scalar.activation(padx[b][:, 1:5, 1:65], ps[:, bank, 0:T].rearrange("p (y x) -> p y x", y=4),
                                         ACT.Copy).then_inc(R[name].sem, 1)
                    if with_ctx:
                        nc.scalar.activation(padc[b][:, 1:257], ps[:, bank, T:], ACT.Copy).then_inc(R[name].sem, 1)

                hi(0)
                R["pst_in"].wait(act, i * 16 + 16)
                R["pair_done"].wait(act, i)
                nc.scalar.activation(pp, pst, ACT.Copy).then_inc(R["pst_free"].sem, 1)
                to_pad(0, 0, "pad_k", True, ("conv_r", i * 9), 2)
                hi(1)
                hi(2)
                for d in range(2):
                    R["lora_mm"].wait(act, i * 4 + 2 * d + 1)
                    nc.scalar.activation(TW[:, d, :], ps[:, 4 + d, :], ACT.Tanh, bias=hpar[:, d:d + 1],
                                         scale=0.5).then_inc(R["tw_ok"].sem, 1)
                    R["lora_mm"].wait(act, i * 4 + 2 * d + 2)
                    nc.scalar.activation(TA[:, d, :], ps[:, 6 + d, :], ACT.Tanh, bias=hpar[:, 2 + d:3 + d],
                                         scale=0.5).then_inc(R["ta_ok"].sem, 1)
                hi(3)
                to_pad(2, 0, "pad_r", False, ("conv_k", i * 12 + 12), 4)
                R["kk"].wait(act, i + 1)
                nc.scalar.activation(ksq, kkn, ACT.Square).then_inc(R["kksq"].sem, 1)
                hi(4)
                R["cw"].wait(act, i * 2 + 2)
                nc.scalar.activation(PD, CW, ACT.Exp).then_inc(R["exps"].sem, 1)
                nc.scalar.activation(KA, CW, ACT.Exp, scale=-1.0).then_inc(R["exps"].sem, 1)
                R["cwm"].wait(act, i + 1)
                nc.scalar.activation(AR[:, :, 0, :], TW, ACT.Exp).then_inc(R["exps"].sem, 1)
                R["nrm_mm"].wait(act, i + 1)
                nc.scalar.activation(ksq, ps[:, 0, :], ACT.Ln, bias=kst_[:, 0:1]).then_inc(R["lnn"].sem, 1)
                R["lnn"].wait(act, i + 1)
                nc.scalar.activation(ksq, ksq, ACT.Exp, scale=-0.5).then_inc(R["rsn"].sem, 1)
                hi(5)
                to_pad(1, 1, "pad_v", True, ("conv_v", i * 12), 6)
                hi(6)
                act.wait_ge(unit_used, i * U_PAIR + (S_PAIR + 8))
                nc.scalar.activation(zs, ps[:, 3, 0:T], ACT.Tanh, scale=0.5).then_inc(R["tz"].sem, 1)
                hi(7)
                R["bt_mm"].wait(act, i + 1)
                nc.scalar.activation(tok1, ps[:, 4:6, :].rearrange("p b n -> p (b n)"), ACT.Copy).then_inc(R["bt_ok"].sem, 1)
                R["vt_mm"].wait(act, i + 1)
                nc.scalar.activation(VT, ps[:, 2, :].rearrange("p (c f) -> p c f", c=4), ACT.Copy).then_inc(R["vt_ok"].sem, 1)
                R["kt_mm"].wait(act, i + 1)
                nc.scalar.activation(tok2, ps[:, 0:2, :].rearrange("p b n -> p (b n)"), ACT.Copy).then_inc(R["kt_ok"].sem, 1)
                for n in range(20):
                    d = n % 2
                    R["y_lvl"].wait(act, i * 20 + n + 1)
                    if n >= 2:
                        R["xta_mm"].wait(act, i * 20 + n - 1)
                    nc.scalar.activation(CW[:, d, :], ps[:, 4 + d, :], ACT.Copy).then_inc(R["y_ev"].sem, 1)
                R["wv_mm"].wait(act, i + 1)
                nc.scalar.activation(WV, ps[:, 0:2, :].rearrange("p d (c f) -> p d c f", c=4), ACT.Copy)\
                    .then_inc(R["wv_ok"].sem, 1)
                R["y0_mm"].wait(act, i + 1)
                nc.scalar.activation(ysum, ps[:, 7, 0:T], ACT.Copy).then_inc(R["y0_ok"].sem, 1)
                R["dev_ok"].wait(act, i + 1)
                nc.scalar.activation(ytmp, ydev, ACT.Square).then_inc(R["dsq"].sem, 1)
                R["var_mm"].wait(act, i + 1)
                nc.scalar.activation(yrs, ps[:, 5, 0:T], ACT.Ln, bias=kst_[:, 1:2], scale=1.0 / C).then_inc(R["lnv"].sem, 1)
                R["lnv"].wait(act, i + 1)
                nc.scalar.activation(yrs, yrs, ACT.Exp, scale=-0.5).then_inc(R["rsv"].sem, 1)

        def pool_pairs(pool):
            for b in range(2):
                nc.gpsimd.memset(padx[b], 0.0).then_inc(R["pad_zero"].sem, 1)
                nc.gpsimd.memset(padc[b], 0.0).then_inc(R["pad_zero"].sem, 1)
            with pool.Fori(0, PAIRS) as i:
                for k in range(U_PAIR):
                    split_lo(pool, (S_PAIR + k + LEAD) % RING, (i, U_PAIR, S_PAIR + k + LEAD))
                R["ev_mb"].wait(pool, 2 * i + 2)
                for h in range(2):
                    for lv in range(1, 6):
                        for d in range(2):
                            if h or lv > 1:
                                R["y_lvl"].wait(pool, i * 20 + h * 10 + (lv - 2) * 2 + d + 1)
                            nc.gpsimd.tensor_tensor(diagonal(MKL, d), twice(MB[:, h, d]), lmask(lv, d), ALU.mult)\
                                .then_inc(R["lvl_m"].sem, 1)
                        if lv == 1:
                            if h == 0:
                                R["kt_mm"].wait(pool, i + 1)
                            for d in range(2):
                                if h:
                                    R["xtf"].wait(pool, i * 8 + 2 * d + 2)
                                nc.gpsimd.tensor_tensor(diagonal(XT, d), twice(MB[:, h, d]), lmask(0, d), ALU.mult)\
                                    .then_inc(R["ev_xt1"].sem, 1)

        def lmask(lv, d):
            return level[:, lv, d].unsqueeze(1).broadcast_to([P, 4, 2, C])

        def twice(v):
            return v.unsqueeze(2).broadcast_to([P, 4, 2, C])

        def diagonal(V, d):
            return V[:, d].rearrange("p c (b t) -> p c b t", b=2)

        def bc2(mask, a, b):
            return mask.unsqueeze(1).unsqueeze(1).broadcast_to([P, a, b, C])

        def dve_pairs(dve):
            nc.vector.memset(kst_[:, 0:1], 1e-12).then_inc(R["kconst"].sem, 1)
            nc.vector.memset(kst_[:, 1:2], LN_EPS).then_inc(R["kconst"].sem, 1)
            nc.vector.memset(kst_[:, 2:3], 1.0).then_inc(R["kconst"].sem, 1)
            R["kconst"].wait(dve, 3)
            with dve.Fori(0, PAIRS) as i:
                def conv(b, src, out, done, ready, taps, with_ctx, bank_w):
                    R[ready[0]].wait(dve, ready[1])
                    n = 12 if with_ctx else 9
                    ox = out[:, 0:T].rearrange("p (y x) -> p y x", y=4)
                    for k in range(9):
                        win = padx[b][:, k // 3:k // 3 + 4, k % 3:k % 3 + 64]
                        w = pp[:, bank_w + k:bank_w + k + 1]
                        if k == 0:
                            nc.vector.tensor_scalar(ox, win, w, None, ALU.mult).then_inc(R[done].sem, 1)
                        else:
                            R[done].wait(dve, i * n + (k + max(0, min(k - 1, 3)) if with_ctx else k))
                            nc.vector.scalar_tensor_tensor(ox, win, w, ox, ALU.mult, ALU.add).then_inc(R[done].sem, 1)
                        if with_ctx and 1 <= k <= 3:
                            win = padc[b][:, k - 1:k + 255]
                            w = pp[:, bank_w + 2 + k:bank_w + 3 + k]
                            oc = out[:, T:]
                            if k == 1:
                                nc.vector.tensor_scalar(oc, win, w, None, ALU.mult).then_inc(R[done].sem, 1)
                            else:
                                R[done].wait(dve, i * n + 2 * k)
                                nc.vector.scalar_tensor_tensor(oc, win, w, oc, ALU.mult, ALU.add).then_inc(R[done].sem, 1)
                    R[done].wait(dve, i * n + n)

                R["pst_free"].wait(dve, i + 1)
                nc.vector.tensor_scalar(hpar[:, 0:4], pp[:, PP["w0"]:PP["w0"] + 4], 0.5, None, ALU.mult).then_inc(R["hp"].sem, 1)
                nc.vector.tensor_scalar(hpar[:, 4:5], pp[:, PP["k_a"]:PP["k_a"] + 1], 0.5, None, ALU.mult)\
                    .then_inc(R["kconst"].sem, 1)
                R["kconst"].wait(dve, i * 2 + 4)
                nc.vector.tensor_scalar(hpar[:, 5:6], hpar[:, 4:5], -1.0, 1.0, ALU.mult, ALU.add).then_inc(R["kconst"].sem, 1)
                conv(0, None, kc, "conv_k", ("pad_k", 2 * i + 2), 0, True, PP["k"])
                nc.vector.tensor_scalar(kkn, kc, pp[:, PP["k_k"]:PP["k_k"] + 1], None, ALU.mult).then_inc(R["kk"].sem, 1)
                R["tw_ok"].wait(dve, 2 * i + 2)
                nc.vector.tensor_scalar(TW, TW, -DECAY / 2, -DECAY / 2, ALU.mult, ALU.add).then_inc(R["logw"].sem, 1)
                R["logw"].wait(dve, i + 1)
                nc.vector.tensor_tensor_scan(CW[:, 0, :], keep[:, 0], TW[:, 0, :], 0.0, ALU.mult, ALU.add)\
                    .then_inc(R["cw"].sem, 1)
                nc.vector.tensor_tensor_scan(CW[:, 1, ::-1], keep[:, 1, ::-1], TW[:, 1, ::-1], 0.0, ALU.mult, ALU.add)\
                    .then_inc(R["cw"].sem, 1)
                R["cw"].wait(dve, 2 * i + 2)
                nc.vector.tensor_tensor(TW, CW, TW, ALU.subtract).then_inc(R["cwm"].sem, 1)
                conv(0, None, rc, "conv_r", ("pad_r", i + 1), 0, False, PP["r"])
                R["rsn"].wait(dve, i + 1)
                R["kk"].wait(dve, i + 1)
                nc.vector.tensor_tensor(kkn, kkn, ksq, ALU.mult).then_inc(R["kkn_ok"].sem, 1)
                R["kkn_ok"].wait(dve, i + 1)
                kk2 = kkn.unsqueeze(1).broadcast_to([P, 2, 512])
                R["exps"].wait(dve, i * 3 + 3)
                nc.vector.scalar_tensor_tensor(AR[:, :, 0, :], AR[:, :, 0, :], -1.0, kk2, ALU.mult, ALU.mult)\
                    .then_inc(R["ar_ok"].sem, 1)
                R["ta_ok"].wait(dve, 2 * i + 2)
                nc.vector.scalar_tensor_tensor(BE, TA, 1.0, kk2, ALU.add, ALU.mult).then_inc(R["be1"].sem, 1)
                nc.vector.tensor_tensor(AR[:, :, 1, 0:T], PD[:, :, 0:T], rc.unsqueeze(1).broadcast_to([P, 2, T]), ALU.mult)\
                    .then_inc(R["rho_ok"].sem, 1)
                R["be1"].wait(dve, i + 1)
                R["ar_ok"].wait(dve, i + 1)
                nc.vector.scalar_tensor_tensor(BE, BE, 0.5, KA, ALU.mult, ALU.mult).then_inc(R["be_ok"].sem, 1)
                R["kconst"].wait(dve, i * 2 + 5)
                nc.vector.tensor_scalar(TA, TA, hpar[:, 4:5], hpar[:, 5:6], ALU.mult, ALU.add).then_inc(R["kd"].sem, 1)
                R["kd"].wait(dve, i + 1)
                nc.vector.tensor_tensor(TA, TA, kc.unsqueeze(1).broadcast_to([P, 2, 512]), ALU.mult).then_inc(R["kd2"].sem, 1)
                R["kd2"].wait(dve, i + 1)
                nc.vector.tensor_tensor(KA, KA, TA, ALU.mult).then_inc(R["ka_ok"].sem, 1)
                nc.vector.tensor_tensor(bon, TA[:, 0, 0:T], TA[:, 1, 0:T], ALU.add).then_inc(R["bon1"].sem, 1)
                R["bon1"].wait(dve, i + 1)
                nc.vector.scalar_tensor_tensor(bon, bon, pp[:, PP["r_k"]:PP["r_k"] + 1], rc, ALU.mult, ALU.mult)\
                    .then_inc(R["bon_ok"].sem, 1)
                R["tz"].wait(dve, i + 1)
                nc.vector.scalar_tensor_tensor(zs, zs, 1.0, ps[:, 3, 0:T], ALU.add, ALU.mult).then_inc(R["z_ok"].sem, 1)
                conv(1, None, vc, "conv_v", ("pad_v", 2 * i + 2), 0, True, PP["v"])
                def masked(bank, out, mm, mask, signal):
                    R[mm].wait(dve, i + 1)
                    b5 = ps[:, bank:bank + 2, :].rearrange("p h (d c t) -> p h d c t", d=2, c=4)
                    for d in range(2):
                        nc.vector.tensor_tensor(out[:, :, d], b5[:, :, d], bc2(mask(d), 2, 4), ALU.mult)\
                            .then_inc(R[signal].sem, 1)

                masked(4, MB, "prod_b", lambda d: strict[:, d], "ev_mb")
                def first_x(h, d):
                    nc.vector.tensor_tensor(diagonal(X, d), twice(ps[:, 2 + h, d * T:d * T + T].rearrange("p (c t) -> p c t", c=4)),
                                            lmask(0, 1 - d), ALU.mult).then_inc(R["ev_x1"].sem, 1)

                def add_eye(V, h, before, signal):
                    for d in range(2):
                        R[before].wait(dve, i * 4 + 2 * h + d + 1)
                        nc.vector.tensor_tensor(V[:, d], V[:, d], ident.unsqueeze(1).broadcast_to([P, 4, P]), ALU.add)\
                            .then_inc(R[signal].sem, 1)

                R["prod_a"].wait(dve, i + 1)
                for d in range(2):
                    first_x(0, d)
                add_eye(X, 0, "ev_x1", "ev_x")
                masked(0, MK, "prod_k", lambda d: strict[:, d], "ev_mk")
                R["prod_q"].wait(dve, i + 1)
                b6 = ps[:, 6:8, :].rearrange("p h (b d c t) -> p (h b) d c t", b=2, d=2, c=2)
                q6 = BKR.rearrange("p (x d c t) -> p x d c t", x=4, d=2, c=2)
                for d in range(2):
                    nc.vector.tensor_tensor(q6[:, :, d], b6[:, :, d], bc2(incl[:, d], 4, 2), ALU.mult)\
                        .then_inc(R["ev_q"].sem, 1)
                add_eye(XT, 0, "ev_xt1", "ev_xt")
                for h in range(2):
                    for n in range(8):
                        d = n % 2
                        R["xa_mm"].wait(dve, i * 16 + h * 8 + n + 1)
                        if n < 2:
                            R["ev_x"].wait(dve, i * 4 + 2 * h + d + 1)
                            R["ev_xt"].wait(dve, i * 4 + 2 * h + d + 1)
                        nc.vector.tensor_tensor(TA[:, d, :], ps[:, 6 + d, :], TA[:, d, :], ALU.add)\
                            .then_inc(R["x_up"].sem, 1)
                        R["xta_mm"].wait(dve, i * 20 + h * 10 + n + 1)
                        nc.vector.tensor_tensor(KA[:, d, :], ps[:, d, :], KA[:, d, :], ALU.add)\
                            .then_inc(R["xt_up"].sem, 1)
                    if h == 0:
                        R["x_up"].wait(dve, i * 16 + 8)
                        for d in range(2):
                            R["y_lvl"].wait(dve, i * 20 + 8 + d + 1)
                            first_x(1, d)
                        add_eye(X, 1, "ev_x1", "ev_x")
                    R["xt_up"].wait(dve, i * 16 + h * 8 + 8)
                    for d in range(2):
                        R["xta_mm"].wait(dve, i * 20 + h * 10 + 8 + d + 1)
                        for p in parts:
                            nc.vector.tensor_tensor(XTF[p, h, d], ps[p, d, :].rearrange("p (c t) -> p c t", c=4)[:, :, p],
                                                    XT[p, d, :, p], ALU.add).then_inc(R["xtf"].sem, 1)
                    if h == 0:
                        add_eye(XT, 1, "ev_xt1", "ev_xt")
                for q in range(8):
                    halves = [slice(C * (ORDER[d][q] % 2), C * (ORDER[d][q] % 2) + C) for d in range(2)]
                    ends = [C * ORDER[d][q] + (C - 1 if d == 0 else 0) for d in range(2)]
                    for d in range(2):
                        tk, tile = halves[d], ORDER[d][q] // 2
                        if q:
                            R["rhs_mm"].wait(dve, i * 14 + 2 * (q - 1) + d + 1)
                            nc.vector.tensor_tensor(RR[tk].rearrange("p (h v) -> p h v", h=2), ps[tk, 4:6, 0:C],
                                                    WV[tk, d, tile].rearrange("p (h v) -> p h v", h=2), ALU.add)\
                                .then_inc(R["rhs_ev"].sem, 1)
                        else:
                            if d == 0:
                                R["wv_ok"].wait(dve, i + 1)
                            nc.vector.tensor_copy(RR[tk], WV[tk, d, tile]).then_inc(R["rhs_ev"].sem, 1)
                    if 0 < q < 7:
                        for d in range(2):
                            R["st_ok"].wait(dve, i * 14 + 2 * (q - 1) + d + 1)
                            nc.vector.tensor_scalar(SP_[:, d], ST[:, q % 2, d], PD[:, d, ends[d]:ends[d] + 1], None,
                                                    ALU.mult).then_inc(R["sp_ok"].sem, 1)
                    for d in range(2):
                        R["u_mm"].wait(dve, i * 16 + 2 * q + d + 1)
                        nc.vector.tensor_copy(UU[halves[d]], ps[halves[d], 6, 0:P]).then_inc(R["u_ev"].sem, 1)
                    if q < 7:
                        for d in range(2):
                            R["ds_mm"].wait(dve, i * 14 + 2 * q + d + 1)
                            new = ST[:, (q + 1) % 2, d]
                            src = ps[:, 2 + d, 0:C]
                            dec = PD[:, d, ends[d]:ends[d] + 1]
                            if q == 0:
                                nc.vector.tensor_scalar(new, src, dec, None, ALU.mult).then_inc(R["st_ok"].sem, 1)
                            else:
                                R["sp_ok"].wait(dve, i * 12 + 2 * (q - 1) + d + 1)
                                nc.vector.scalar_tensor_tensor(new, src, dec, SP_[:, d], ALU.mult, ALU.add)\
                                    .then_inc(R["st_ok"].sem, 1)
                R["y0_ok"].wait(dve, i + 1)
                nc.vector.tensor_tensor(ysum, ps[:, 7, T:], ysum, ALU.add).then_inc(R["y0a"].sem, 1)
                R["y0a"].wait(dve, i + 1)
                R["yo_mm"].wait(dve, i * 4 + 4)
                nc.vector.tensor_tensor(ysum, ps[:, 0, 0:T], ysum, ALU.add).then_inc(R["y0b"].sem, 1)
                R["y0b"].wait(dve, i + 1)
                nc.vector.tensor_tensor(ysum, ps[:, 1, 0:T], ysum, ALU.add).then_inc(R["ys_ok"].sem, 1)
                R["bonus_mm"].wait(dve, i + 1)
                nc.vector.tensor_tensor(bon, ps[:, 6, 0:T], vc[:, 0:T], ALU.mult).then_inc(R["y1"].sem, 1)
                R["mean_mm"].wait(dve, i + 1)
                nc.vector.scalar_tensor_tensor(ydev, ps[:, 4, 0:T], -1.0 / C, ysum, ALU.mult, ALU.add)\
                    .then_inc(R["dev_ok"].sem, 1)
                R["rsv"].wait(dve, i + 1)
                nc.vector.tensor_tensor(ydev, ydev, yrs, ALU.mult).then_inc(R["y2"].sem, 1)
                R["y2"].wait(dve, i + 1)
                nc.vector.tensor_scalar(ydev, ydev, pp[:, PP["ln_g"]:PP["ln_g"] + 1], pp[:, PP["ln_b"]:PP["ln_b"] + 1],
                                        ALU.mult, ALU.add).then_inc(R["y3"].sem, 1)
                R["y3"].wait(dve, i + 1)
                nc.vector.tensor_tensor(ydev, ydev, bon, ALU.add).then_inc(R["y4"].sem, 1)
                R["y4"].wait(dve, i + 1)
                nc.vector.scalar_tensor_tensor(YA[:, bass.ds(i, 1), :].rearrange("p a t -> p (a t)"), ydev, 0.5, zs,
                                               ALU.mult, ALU.mult).then_inc(R["pair_done"].sem, 1)

        place[0] = 2048
        YB = area(KT // 2 * T).rearrange("p (k t) -> p k t", t=T)
        VF = area(1024)
        GL = area(1024).rearrange(dd, d=2)
        GE = area(1024).rearrange(dd, d=2)
        GC = area(1024).rearrange(dd, d=2)
        QD = area(512).rearrange(dd, d=2)
        KI = area(512).rearrange(dd, d=2)
        KS = area(1024).rearrange(dd, d=2)
        VTG = area(1024).rearrange("p (c f) -> p c f", c=4)
        KST = area(1024).rearrange("p (d c f) -> p d c f", d=2, c=4)
        AT = area(512).rearrange("p (d c t) -> p d c t", d=2, c=2)
        SG = area(1024).rearrange("p (b d v) -> p b d v", b=2, d=2)
        zg = area(512)
        sqg = area(512)
        rsg = area(256)
        DEC = area(16).rearrange("p (d c) -> p d c", d=2)
        gkw_all = area(1024)
        gkw = area(256)
        gbias = area(4)
        gmask = cns[:, CN["gmask"]].rearrange("p (d t) -> p d t", d=2)
        names = ("gw_in=16 gw_ok:2 vf_ok:1 gabs:2 gexp:1 gln:1 gl1:2 gl2:1 gc:2 dif:2 eq:1 ekn:1 eks:1 dec:2 "
                 "qd_ok:1 ki_ok:1 ks_ok:1 att_mm:1 at_ok:2 gk_mm:2 vt_mm:1 vt_ok:1 kst_mm:1 kst_ok:1 ds_mm:7 "
                 "st_ok:14 o_step:3 o_mm:1 tz:1 z_ok:1 sq:1 ms_mm:1 lns:1 rs:1 y1:2 head_done:1 const=6")
        retire(R)
        G = counts("g", names, GH)

        def pe_gla(pe):
            R["pair_done"].wait(pe, PAIRS)
            with pe.Fori(0, GH) as i:
                def tile(k, out, sel):
                    mm_tile(pe, S_GLA, i, U_GLA, k, out, sel)
                tile(0, ps[:, 2, :], both)
                G["head_done"].wait(pe, i)
                G["gw_ok"].wait(pe, 2 * i + 2)
                for d in range(2):
                    nc.tensor.matmul(ps[:, 5 + d, :], gkw[0:32, P * d:P * d + P], LG[:, :], start=True, stop=True)\
                        .then_inc(G["gk_mm"].sem, 1)
                tile(2, ps[:, 0, 0:T], 0)
                tile(4, ps[:, 1, :], both)
                tile(6, ps[:, 3, :], both)
                tile(8, ps[:, 4, 0:T], 0)
                G["qd_ok"].wait(pe, i + 1)
                G["ki_ok"].wait(pe, i + 1)
                for d in range(2):
                    for c in range(2):
                        t = slice(P * c, P * c + P)
                        ins = nc.tensor.matmul(ps[:, 7, (2 * d + c) * P:(2 * d + c) * P + P], KI[:, d, t], QD[:, d, t],
                                               start=True, stop=True)
                ins.then_inc(G["att_mm"].sem, 1)
                tile(10, ps[:, 4, T:], 0)
                G["vf_ok"].wait(pe, i + 1)
                G["gl1"].wait(pe, 2 * i + 2)
                for c in range(4):
                    for m in range(2):
                        o = (c % 2) * T + m * P
                        ins = nc.tensor.transpose(ps[:, 5 + c // 2, o:o + P], VF[:, m * 512 + c * P:m * 512 + c * P + P],
                                                  ident)
                ins.then_inc(G["vt_mm"].sem, 1)
                G["ks_ok"].wait(pe, i + 1)
                for d in range(2):
                    for c in range(4):
                        ins = nc.tensor.transpose(ps[:, 2 + d, c * P:c * P + P], KS[:, d, c * P:c * P + P], ident)
                ins.then_inc(G["kst_mm"].sem, 1)
                G["at_ok"].wait(pe, 2 * i + 2)
                G["vt_ok"].wait(pe, i + 1)
                for m in range(2):
                    for d in range(2):
                        for c in range(2):
                            nc.tensor.matmul(ps[:, m, P * c:P * c + P], VTG[:, c, m * P:m * P + P], AT[:, d, c],
                                             start=d == 0 and c == 0, stop=False, skip_group_check=True)
                G["kst_ok"].wait(pe, i + 1)
                def addition(q):
                    if q >= 2:
                        G["st_ok"].wait(pe, i * 14 + 2 * q - 2)
                    for d in range(2):
                        c = ORDER[d][q]
                        tk = slice(C * (c % 2), C * (c % 2) + C)
                        ins = nc.tensor.matmul(ps[:, (2, 5)[q % 2] + d, 0:T], KST[tk, d, c // 2], VTG[tk, c // 2, :],
                                               start=True, stop=True)
                    ins.then_inc(G["ds_mm"].sem, 1)

                addition(0)
                for q in range(8):
                    if q < 6:
                        addition(q + 1)
                    if q >= 4:
                        G["st_ok"].wait(pe, i * 14 + 2 * q)
                        for d in range(2):
                            c = ORDER[d][q]
                            for m in range(2):
                                ins = nc.tensor.matmul(ps[:, m, C * c:C * c + C], SG[:, q % 2, d, m * P:m * P + P],
                                                       QD[:, d, C * c:C * c + C], start=False, stop=q == 7 and d == 1,
                                                       skip_group_check=True)
                        if q < 7:
                            ins.then_inc(G["o_step"].sem, 1)
                ins.then_inc(G["o_mm"].sem, 1)
                G["sq"].wait(pe, i + 1)
                for m in range(2):
                    ins = nc.tensor.matmul(ps[:, 7, 0:T], meanw, sqg[:, m * T:m * T + T], start=m == 0, stop=m == 1)
                ins.then_inc(G["ms_mm"].sem, 1)

        def act_gla(act):
            R["pair_done"].wait(act, PAIRS)
            act.dma_start(gkw_all[0:32, :], gk_w.rearrange("r d n -> r (d n)")).then_inc(G["gw_in"].sem, 16)
            with act.Fori(0, GH) as i:
                def hi(*ks):
                    for k in ks:
                        split_hi(act, (S_GLA + k + LEAD) % RING, (i, U_GLA, S_GLA + k + LEAD))

                hi(0, 1)
                G["gk_mm"].wait(act, 2 * i + 2)
                G["head_done"].wait(act, i)
                hi(2)
                for d in range(2):
                    nc.scalar.activation(GE[:, d, :], ps[:, 5 + d, :], ACT.Abs, bias=gbias[:, d:d + 1])\
                        .then_inc(G["gabs"].sem, 1)
                G["gabs"].wait(act, 2 * i + 2)
                nc.scalar.activation(GE, GE, ACT.Exp, scale=-1.0).then_inc(G["gexp"].sem, 1)
                G["gexp"].wait(act, i + 1)
                nc.scalar.activation(GE, GE, ACT.Ln, bias=kst_[:, 2:3]).then_inc(G["gln"].sem, 1)
                hi(3, 4)
                G["gc"].wait(act, 2 * i + 2)
                nc.scalar.activation(QD, GC[:, :, 0:T], ACT.Exp, scale=1.0 / 16).then_inc(G["eq"].sem, 1)
                nc.scalar.activation(KI, GC[:, :, 0:T], ACT.Exp, scale=-1.0 / 16).then_inc(G["ekn"].sem, 1)
                for d in range(2):
                    end = GC[:, d, (C - 1 if d == 0 else 0)::C]
                    nc.scalar.activation(DEC[:, d, :], end, ACT.Exp, scale=1.0 / 16).then_inc(G["dec"].sem, 1)
                G["dif"].wait(act, 2 * i + 2)
                nc.scalar.activation(KS, KS, ACT.Exp, scale=1.0 / 16).then_inc(G["eks"].sem, 1)
                hi(5)
                act.wait_ge(unit_used, i * U_GLA + (S_GLA + 8))
                nc.scalar.activation(VF, ps[:, 2:4, :].rearrange("p b n -> p (b n)"), ACT.Copy).then_inc(G["vf_ok"].sem, 1)
                hi(6, 7, 8)
                act.wait_ge(unit_used, i * U_GLA + (S_GLA + 12))
                nc.scalar.activation(zg, ps[:, 4, :], ACT.Tanh, scale=0.5).then_inc(G["tz"].sem, 1)
                G["vt_mm"].wait(act, i + 1)
                nc.scalar.activation(VTG.rearrange("p c f -> p (c f)"), ps[:, 5:7, :].rearrange("p b n -> p (b n)"),
                                     ACT.Copy).then_inc(G["vt_ok"].sem, 1)
                G["kst_mm"].wait(act, i + 1)
                nc.scalar.activation(KST.rearrange("p d c f -> p (d c f)"), ps[:, 2:4, :].rearrange("p b n -> p (b n)"),
                                     ACT.Copy).then_inc(G["kst_ok"].sem, 1)
                hi(9, 10, 11)
                G["o_mm"].wait(act, i + 1)
                nc.scalar.activation(sqg.rearrange("p (m t) -> p m t", m=2), ps[:, 0:2, 0:T], ACT.Square)\
                    .then_inc(G["sq"].sem, 1)
                G["ms_mm"].wait(act, i + 1)
                nc.scalar.activation(rsg, ps[:, 7, 0:T], ACT.Ln, bias=kst_[:, 3:4], scale=KT * P / 256.0)\
                    .then_inc(G["lns"].sem, 1)
                G["lns"].wait(act, i + 1)
                nc.scalar.activation(rsg, rsg, ACT.Exp, scale=-0.5).then_inc(G["rs"].sem, 1)

        def pool_gla(pool):
            with pool.Fori(0, GH) as i:
                for k in range(U_GLA):
                    split_lo(pool, (S_GLA + k + LEAD) % RING, (i, U_GLA, S_GLA + k + LEAD))

        def dve_gla(dve):
            nc.vector.memset(kst_[:, 3:4], EPS).then_inc(G["const"].sem, 1)
            nc.vector.tensor_scalar(small[:, 68:70], pv[:, PV["b_norm_g"]], 0.5, None, ALU.mult).then_inc(G["const"].sem, 1)
            G["const"].wait(dve, 2)
            R["pair_done"].wait(dve, PAIRS)
            G["gw_in"].wait(dve, 16)
            gk_b = pv[:, PV["gk_b"]].rearrange("p (d g) -> p d g", d=2)
            gw4 = gkw_all.rearrange("p (d n) -> p d n", d=2)
            with dve.Fori(0, GH) as i:
                nc.vector.tensor_copy(gkw[0:32, :].rearrange("p (d n) -> p d n", d=2), gw4[0:32, :, bass.ds(i * P, P)])\
                    .then_inc(G["gw_ok"].sem, 1)
                nc.vector.tensor_copy(gbias[:, 0:2].unsqueeze(2), gk_b[:, :, bass.ds(i, 1)]).then_inc(G["gw_ok"].sem, 1)
                G["gw_ok"].wait(dve, 2 * i + 2)
                G["gabs"].wait(dve, 2 * i + 2)
                for d in range(2):
                    nc.vector.tensor_scalar(GL[:, d, :], ps[:, 5 + d, :], gbias[:, d:d + 1], 0.0, ALU.add, ALU.min)\
                        .then_inc(G["gl1"].sem, 1)
                G["gl1"].wait(dve, 2 * i + 2)
                G["gln"].wait(dve, i + 1)
                nc.vector.tensor_tensor(GL, GL, GE, ALU.subtract).then_inc(G["gl2"].sem, 1)
                G["gl2"].wait(dve, i + 1)
                nc.vector.tensor_tensor_scan(GC[:, 0, :], keep[:, 0], GL[:, 0, :], 0.0, ALU.mult, ALU.add)\
                    .then_inc(G["gc"].sem, 1)
                nc.vector.tensor_tensor_scan(GC[:, 1, ::-1], keep[:, 1, ::-1], GL[:, 1, ::-1], 0.0, ALU.mult, ALU.add)\
                    .then_inc(G["gc"].sem, 1)
                G["gc"].wait(dve, 2 * i + 2)
                for d in range(2):
                    g3 = GC[:, d, :].rearrange("p (c t) -> p c t", t=C)
                    e = C - 1 if d == 0 else 0
                    nc.vector.tensor_tensor(KS[:, d, :].rearrange("p (c t) -> p c t", t=C),
                                            g3[:, :, e:e + 1].broadcast_to([P, 8, C]), g3, ALU.subtract)\
                        .then_inc(G["dif"].sem, 1)
                G["eq"].wait(dve, i + 1)
                dve.wait_ge(unit_used, i * U_GLA + (S_GLA + 4))
                nc.vector.scalar_tensor_tensor(QD, QD, P ** -0.5, ps[:, 0, 0:T].unsqueeze(1).broadcast_to([P, 2, T]),
                                               ALU.mult, ALU.mult).then_inc(G["qd_ok"].sem, 1)
                G["ekn"].wait(dve, i + 1)
                dve.wait_ge(unit_used, i * U_GLA + (S_GLA + 6))
                nc.vector.tensor_tensor(KI, KI, ps[:, 1, 0:T].unsqueeze(1).broadcast_to([P, 2, T]), ALU.mult)\
                    .then_inc(G["ki_ok"].sem, 1)
                G["eks"].wait(dve, i + 1)
                nc.vector.tensor_tensor(KS, KS, ps[:, 1, :].unsqueeze(1).broadcast_to([P, 2, 512]), ALU.mult)\
                    .then_inc(G["ks_ok"].sem, 1)
                G["att_mm"].wait(dve, i + 1)
                for d in range(2):
                    nc.vector.scalar_tensor_tensor(AT[:, d], ps[:, 7, d * T:d * T + T].rearrange("p (c t) -> p c t", c=2),
                                                   3e38, gmask[:, d].unsqueeze(1).broadcast_to([P, 2, P]), ALU.min,
                                                   ALU.mult).then_inc(G["at_ok"].sem, 1)
                G["tz"].wait(dve, i + 1)
                nc.vector.scalar_tensor_tensor(zg, zg, 1.0, ps[:, 4, :], ALU.add, ALU.mult).then_inc(G["z_ok"].sem, 1)
                G["dec"].wait(dve, 2 * i + 2)
                for q in range(7):
                    G["ds_mm"].wait(dve, i * 7 + q + 1)
                    if q >= 5:
                        G["o_step"].wait(dve, i * 3 + q - 4)
                    for d in range(2):
                        c = ORDER[d][q]
                        new = SG[:, (q + 1) % 2, d, :]
                        add = ps[:, (2, 5)[q % 2] + d, 0:T]
                        if q == 0:
                            nc.vector.tensor_copy(new, add).then_inc(G["st_ok"].sem, 1)
                        else:
                            G["st_ok"].wait(dve, i * 14 + 2 * (q - 1) + d + 1)
                            nc.vector.scalar_tensor_tensor(new, SG[:, q % 2, d, :], DEC[:, d, c:c + 1], add,
                                                           ALU.mult, ALU.add).then_inc(G["st_ok"].sem, 1)
                G["rs"].wait(dve, i + 1)
                G["z_ok"].wait(dve, i + 1)
                for m in range(2):
                    nc.vector.tensor_tensor(sqg[:, m * T:m * T + T], ps[:, m, 0:T], rsg, ALU.mult).then_inc(G["y1"].sem, 1)
                G["y1"].wait(dve, 2 * i + 2)
                for m in range(2):
                    ins = nc.vector.scalar_tensor_tensor(YB[:, bass.ds(2 * i + m, 1), :].rearrange("p a t -> p (a t)"),
                                                         sqg[:, m * T:m * T + T], small[:, 68 + m:69 + m],
                                                         zg[:, m * T:m * T + T], ALU.mult, ALU.mult)
                    if m == 1:
                        ins.then_inc(G["head_done"].sem, 1)
                    else:
                        ins.then_inc(G["const"].sem, 1)

        M = counts("m", "yhi ylo x_in c_in tg m1 m2 mix mhi mlo xr", 1)
        retire(G)
        y16 = W[:, 0:KT * T].rearrange("p (k t) -> p k t", k=KT)

        def act_ysplit(act):
            G["head_done"].wait(act, GH)
            G["const"].wait(act, 2 + GH)
            for k in range(0, KT, 4):
                nc.scalar.activation(ahi[:, 1, k:k + 4, :], y16[:, k:k + 4, :], ACT.Copy).then_inc(M["yhi"].sem, 1)
            M["ylo"].wait(act, 4)
            act.dma_start(XR[:, :, :], xT[:, 0]).then_inc(M["x_in"].sem, 16)
            act.dma_start(cns2[:, :], consts2).then_inc(M["c_in"].sem, 16)

        def dve_ysplit(dve):
            for k in range(0, KT, 4):
                M["yhi"].wait(dve, k // 4 + 1)
                nc.vector.tensor_tensor(alo[:, 1, k:k + 4, :], y16[:, k:k + 4, :], ahi[:, 1, k:k + 4, :].bitcast(F32),
                                        ALU.subtract).then_inc(M["ylo"].sem, 1)

        work_stack.close()
        XR = ctx.enter_context(nc.sbuf_tensor("XR", [P, KT, T], F32))
        cns2 = sb("cns2", NCN2)
        V = ctx.enter_context(nc.sbuf_tensor("V", [P, 5648], F32))
        mix_stack = ExitStack()
        mhi = mix_stack.enter_context(nc.sbuf_tensor("mhi", [P, KT, T], F32R))
        mlo = mix_stack.enter_context(nc.sbuf_tensor("mlo", [P, KT, T], F32R))
        vplace = [0]

        def varea(cols):
            a = vplace[0]
            vplace[0] += cols
            assert vplace[0] <= 5648, vplace[0]
            return V[:, a:a + cols]

        tg = varea(1024).rearrange("p (b n) -> p b n", b=2)
        mx = varea(512).rearrange("p (b n) -> p b n", b=2)

        assert M["mix"].base > 1

        def pe_merge(pe):
            G["head_done"].wait(pe, GH)
            with pe.Fori(0, KT // 2) as i:
                for n in range(2):
                    M["mix"].wait(pe, i * 2 + n - 1)
                    b = S_MERGE + U_MERGE * n
                    bank = 4 * n
                    mm_tile(pe, b, i, 12, 0, ps[:, bank, 0:T], 0)
                    mm_tile(pe, b, i, 12, 2, ps[:, bank + 1, 0:T], 0)
                    M["ylo"].wait(pe, 4)
                    for u in range(2):
                        mm_unit(pe, (b + 4 + u) % RING, i * 12 + (b + 4 + u), ps[:, bank + 2 + u, 0:T], 1, UK * u, True,
                                True)

        def act_merge(act):
            with act.Fori(0, KT // 2) as i:
                def hi(*ks):
                    for k in ks:
                        split_hi(act, (S_MERGE + k + LEAD) % RING, (i, 12, S_MERGE + k + LEAD))
                for n in range(2):
                    k = U_MERGE * n
                    hi(k, k + 1)
                    act.wait_ge(unit_used, i * 12 + (S_MERGE + k + 2))
                    M["m2"].wait(act, i * 2 + n - 1) if n else M["m2"].wait(act, i * 2)
                    nc.scalar.activation(tg[:, n, 0:T], ps[:, 4 * n, 0:T], ACT.Tanh, scale=0.5).then_inc(M["tg"].sem, 1)
                    hi(k + 2, k + 3)
                    act.wait_ge(unit_used, i * 12 + (S_MERGE + k + 4))
                    nc.scalar.activation(tg[:, n, T:], ps[:, 4 * n + 1, 0:T], ACT.Tanh, scale=0.5).then_inc(M["tg"].sem, 1)
                    hi(k + 4, k + 5)
                    M["mix"].wait(act, i * 2 + n + 1)
                    nc.scalar.activation(mhi[:, bass.ds(2 * i + n, 1), :].rearrange("p a t -> p (a t)"), mx[:, n, :],
                                         ACT.Copy).then_inc(M["mhi"].sem, 1)

        def pool_merge(pool):
            pool_stream(pool, S_MERGE, U_MERGE * KT)

        def pool_stream(pool, base, n):
            with pool.Fori(0, n // RING) as i:
                for k in range(RING):
                    split_lo(pool, (base + k + LEAD) % RING, (i, RING, base + k + LEAD))

        def dve_merge(dve):
            with dve.Fori(0, KT // 2) as i:
                for n in range(2):
                    M["tg"].wait(dve, i * 4 + 2 * n + 2)
                    dve.wait_ge(unit_used, i * 12 + (S_MERGE + U_MERGE * n + 6))
                    for g in range(2):
                        nc.vector.scalar_tensor_tensor(tg[:, n, T * g:T * g + T], tg[:, n, T * g:T * g + T], 1.0,
                                                       ps[:, 4 * n + 2 + g, 0:T], ALU.add, ALU.mult)\
                            .then_inc(M["m1"].sem, 1)
                    M["m1"].wait(dve, i * 4 + 2 * n + 2)
                    nc.vector.tensor_tensor(tg[:, n, 0:T], tg[:, n, 0:T], tg[:, n, T:], ALU.add).then_inc(M["m2"].sem, 1)
                    M["m2"].wait(dve, i * 2 + n + 1)
                    nc.vector.tensor_scalar(mx[:, n, :], tg[:, n, 0:T], 0.5, None, ALU.mult).then_inc(M["mix"].sem, 1)
                    M["mix"].wait(dve, i * 2 + n + 1)
                    M["mhi"].wait(dve, i * 2 + n + 1)
                    nsl = bass.ds(2 * i + n, 1)
                    nc.vector.tensor_tensor(mlo[:, nsl, :].rearrange("p a t -> p (a t)"), mx[:, n, :],
                                            mhi[:, nsl, :].rearrange("p a t -> p (a t)").bitcast(F32), ALU.subtract)\
                        .then_inc(M["mlo"].sem, 1)

        def out_phase(name, base, gate, hi_, lo_, sel, ready):
            done = counts(name, "done", 1)["done"]

            def pe_(pe):
                if base == S_OUT1:
                    M["mix"].wait(pe, KT - 1)

                def body(i, n, first=False):
                    if not isinstance(i, int) or i > 0:
                        done.wait(pe, i * 2 + n - 1)
                    for u in range(2):
                        k = base + 2 * n + u
                        mm_unit(pe, k % RING, i * RING + k, ps[:, n, 0:T], sel, UK * u, u == 0, u == 1, hi_, lo_,
                                tile_ready=(lambda t: ready(pe, t)) if first else None)
                for n in range(4):
                    body(n // 2, n % 2, n == 0)
                with pe.Fori(1, KT // 4) as j:
                    for n in range(4):
                        body(j * 2 + n // 2, n % 2)

            def act_(act):
                if base == S_OUT3:
                    with act.Fori(0, KT // 2 - 1) as i:
                        for k in range(RING):
                            split_hi(act, (base + k + LEAD) % RING, (i, RING, base + k + LEAD))
                    for s in range(S_END - RING + LEAD, S_END):
                        split_hi(act, s % RING, s)
                else:
                    with act.Fori(0, KT // 2) as i:
                        for k in range(RING):
                            split_hi(act, (base + k + LEAD) % RING, (i, RING, base + k + LEAD))

            def pool_(pool):
                if base == S_OUT3:
                    pool_stream(pool, base, U_OUT * KT - RING)
                    for s in range(S_END - RING + LEAD, S_END):
                        split_lo(pool, s % RING, s)
                else:
                    pool_stream(pool, base, U_OUT * KT)

            def dve_(dve):
                with dve.Fori(0, KT // 2) as i:
                    for n in range(2):
                        dve.wait_ge(unit_used, i * RING + (base + 2 * n + 2))
                        x = XR[:, bass.ds(2 * i + n, 1), :].rearrange("p a t -> p (a t)")
                        if gate:
                            g = mod_v[:, bass.ds(2 * i + (2 * KT + n), 1), 0]
                            nc.vector.scalar_tensor_tensor(x, ps[:, n, 0:T], g, x, ALU.mult, ALU.add).then_inc(done.sem, 1)
                        else:
                            nc.vector.tensor_tensor(x, ps[:, n, 0:T], x, ALU.add).then_inc(done.sem, 1)
            return pe_, act_, pool_, dve_, done

        sqv = varea(1024).rearrange("p (b t) -> p b t", b=4)
        rsv = varea(256)

        def norm_phase(name, before, gain, split, count):
            N = counts(name, "sq mm ms root rs x hhi hlo", 1)
            g = pv[:, PV[gain]]

            def pe_(pe):
                for k in range(KT):
                    N["sq"].wait(pe, k + 1)
                    nc.tensor.matmul(ps[:, 7, 0:T], meanw, sqv[:, k % 4], start=k == 0, stop=k == KT - 1)\
                        .then_inc(N["mm"].sem, 1)

            def act_(act):
                before[0].wait(act, before[1])
                for k in range(KT):
                    if k >= 4:
                        N["mm"].wait(act, k - 3)
                    nc.scalar.activation(sqv[:, k % 4], XR[:, k, :], ACT.Square).then_inc(N["sq"].sem, 1)
                N["ms"].wait(act, 1)
                nc.scalar.activation(rsv, rsv, ACT.Sqrt).then_inc(N["root"].sem, 1)
                if split:
                    for k in range(KT):
                        N["x"].wait(act, k + 1)
                        nc.scalar.activation(ahi[:, 0, k, :], sqv[:, k % 4], ACT.Copy).then_inc(N["hhi"].sem, 1)

            def dve_(dve):
                before[0].wait(dve, before[1])
                N["mm"].wait(dve, KT)
                nc.vector.tensor_scalar(rsv, ps[:, 7, 0:T], EPS, None, ALU.add).then_inc(N["ms"].sem, 1)
                N["root"].wait(dve, 1)
                nc.vector.reciprocal(rsv, rsv).then_inc(N["rs"].sem, 1)
                N["rs"].wait(dve, 1)
                for k in range(KT):
                    out = sqv[:, k % 4] if split else XR[:, k, :]
                    if split and k >= 4:
                        N["hlo"].wait(dve, k - 3)
                    nc.vector.scalar_tensor_tensor(out, XR[:, k, :], g[:, k:k + 1], rsv, ALU.mult, ALU.mult)\
                        .then_inc(N["x"].sem, 1)

            def pool_(pool):
                for k in range(KT):
                    N["x"].wait(pool, k + 1)
                    N["hhi"].wait(pool, k + 1)
                    nc.gpsimd.tensor_tensor(alo[:, 0, k, :], sqv[:, k % 4], ahi[:, 0, k, :].bitcast(F32), ALU.subtract)\
                        .then_inc(N["hlo"].sem, 1)
            if split:
                return pe_, act_, dve_, pool_, (N["hlo"], KT)
            return pe_, act_, dve_, (N["x"], KT)

        cos, sin = cns2[:, CN2["cos"]], cns2[:, CN2["sin"]]
        rot = varea(512)
        qk = varea(512)
        sm = varea(384)
        smx = varea(8)
        pt = varea(384)
        vf = varea(256)
        vt = varea(256).rearrange("p (c f) -> p c f", c=2)
        zz = varea(256)
        yv = varea(256)
        SC = P ** -0.5

        def rows(v, k):
            return v[:, 0:P] if k == 0 else v[:, P:3 * P]

        def head_phase(name, base, heads, maskname, y0, ready):
            A = counts(name, ("rot t2 t1 qk s_mm sm mx nm p rc pn pt_mm pt_ok vf vt_mm vt_ok o_mm tz "
                                                 "zz y yhi done"), heads)
            mask = cns2[:, CN2[maskname]]

            def pe_(pe):
                with pe.Fori(0, heads) as i:
                    A["t1"].wait(pe, i)
                    mm_tile(pe, base, i, U_HEAD, 0, ps[:, 0, 0:T], 0, tile_ready=lambda k: ready[0].wait(pe, k + 1))
                    mm_tile(pe, base, i, U_HEAD, 2, ps[:, 0, T:], 0)
                    mm_tile(pe, base, i, U_HEAD, 4, ps[:, 1, 0:T], 0)
                    A["qk"].wait(pe, i + 1)
                    nc.tensor.matmul(ps[:, 3, 0:P], qk[:, 0:P], qk[:, T:T + P], start=True, stop=True)
                    nc.tensor.matmul(ps[:, 3, P:3 * P], qk[:, P:T], qk[:, T:], start=True, stop=True)\
                        .then_inc(A["s_mm"].sem, 1)
                    A["zz"].wait(pe, i)
                    mm_tile(pe, base, i, U_HEAD, 6, ps[:, 2, 0:T], 0)
                    A["vf"].wait(pe, i + 1)
                    for c in range(2):
                        ins = nc.tensor.transpose(ps[:, 5, P * c:P * c + P], vf[:, P * c:P * c + P], ident)
                    ins.then_inc(A["vt_mm"].sem, 1)
                    A["pn"].wait(pe, 2 * i + 2)
                    for c in range(3):
                        ins = nc.tensor.transpose(ps[:, 4, P * c:P * c + P], sm[:, P * c:P * c + P], ident)
                    ins.then_inc(A["pt_mm"].sem, 1)
                    A["vt_ok"].wait(pe, i + 1)
                    A["pt_ok"].wait(pe, i + 1)
                    nc.tensor.matmul(ps[:, 6, 0:T], vt[:, 0, :], pt[:, 0:T], start=True, stop=False)
                    nc.tensor.matmul(ps[:, 6, P:T], vt[:, 1, :], pt[:, T:], start=False, stop=True)\
                        .then_inc(A["o_mm"].sem, 1)

            def act_(act):
                with act.Fori(0, heads) as i:
                    def hi(*ks):
                        for k in ks:
                            split_hi(act, (base + k + LEAD) % RING, (i, U_HEAD, base + k + LEAD))
                    hi(0, 1, 2)
                    act.wait_ge(unit_used, i * U_HEAD + (base + 4))
                    A["t2"].wait(act, i)
                    for h in range(2):
                        nc.scalar.activation(rot[64 * h:64 * h + 64, :], ps[64 - 64 * h:128 - 64 * h, 0, :], ACT.Copy)\
                            .then_inc(A["rot"].sem, 1)
                    hi(3)
                    act.wait_ge(unit_used, i * U_HEAD + (base + 6))
                    nc.scalar.activation(vf, ps[:, 1, 0:T], ACT.Copy).then_inc(A["vf"].sem, 1)
                    hi(4)
                    for k in range(2):
                        A["nm"].wait(act, 2 * i + k + 1)
                        nc.scalar.activation(rows(sm, k), rows(sm, k), ACT.Exp, bias=smx[:, 2 + k:3 + k], scale=SC,
                                             accum_out=smx[:, 4 + k:5 + k]).then_inc(A["p"].sem, 1)
                    hi(5)
                    act.wait_ge(unit_used, i * U_HEAD + (base + 8))
                    nc.scalar.activation(zz, ps[:, 2, 0:T], ACT.Tanh, scale=0.5).then_inc(A["tz"].sem, 1)
                    A["vt_mm"].wait(act, i + 1)
                    nc.scalar.activation(vt.rearrange("p c f -> p (c f)"), ps[:, 5, 0:T], ACT.Copy).then_inc(A["vt_ok"].sem, 1)
                    A["pt_mm"].wait(act, i + 1)
                    nc.scalar.activation(pt, ps[:, 4, 0:3 * P], ACT.Copy).then_inc(A["pt_ok"].sem, 1)
                    hi(6, 7)
                    A["y"].wait(act, i + 1)
                    nc.scalar.activation(ahi[:, 1, bass.ds(i + y0, 1), :].rearrange("p a t -> p (a t)"), yv, ACT.Copy)\
                        .then_inc(A["yhi"].sem, 1)

            def dve_(dve):
                with dve.Fori(0, heads) as i:
                    A["rot"].wait(dve, 2 * i + 2)
                    A["done"].wait(dve, i)
                    nc.vector.tensor_tensor(rot, rot, sin, ALU.mult).then_inc(A["t2"].sem, 1)
                    nc.vector.tensor_tensor(qk, ps[:, 0, :], cos, ALU.mult).then_inc(A["t1"].sem, 1)
                    A["t1"].wait(dve, i + 1)
                    A["t2"].wait(dve, i + 1)
                    nc.vector.tensor_tensor(qk, qk, rot, ALU.add).then_inc(A["qk"].sem, 1)
                    A["s_mm"].wait(dve, i + 1)
                    nc.vector.tensor_tensor(sm, ps[:, 3, 0:3 * P], mask, ALU.add).then_inc(A["sm"].sem, 1)
                    A["sm"].wait(dve, i + 1)
                    for k in range(2):
                        nc.vector.tensor_reduce(smx[:, k:k + 1], rows(sm, k), AX.X, ALU.max).then_inc(A["mx"].sem, 1)
                    for k in range(2):
                        A["mx"].wait(dve, 2 * i + 2)
                        nc.vector.tensor_scalar(smx[:, 2 + k:3 + k], smx[:, k:k + 1], -SC, None, ALU.mult)\
                            .then_inc(A["nm"].sem, 1)
                    A["p"].wait(dve, 2 * i + 2)
                    nc.vector.reciprocal(smx[:, 6:8], smx[:, 4:6]).then_inc(A["rc"].sem, 1)
                    A["rc"].wait(dve, i + 1)
                    for k in range(2):
                        nc.vector.tensor_scalar(rows(sm, k), rows(sm, k), smx[:, 6 + k:7 + k], None, ALU.mult)\
                            .then_inc(A["pn"].sem, 1)
                    A["tz"].wait(dve, i + 1)
                    nc.vector.scalar_tensor_tensor(zz, zz, 1.0, ps[:, 2, 0:T], ALU.add, ALU.mult).then_inc(A["zz"].sem, 1)
                    A["zz"].wait(dve, i + 1)
                    A["o_mm"].wait(dve, i + 1)
                    nc.vector.scalar_tensor_tensor(yv, ps[:, 6, 0:T], 0.5, zz, ALU.mult, ALU.mult).then_inc(A["y"].sem, 1)
                    A["y"].wait(dve, i + 1)
                    A["yhi"].wait(dve, i + 1)
                    nsl = bass.ds(i + y0, 1)
                    nc.vector.tensor_tensor(alo[:, 1, nsl, :].rearrange("p a t -> p (a t)"), yv,
                                            ahi[:, 1, nsl, :].rearrange("p a t -> p (a t)").bitcast(F32), ALU.subtract)\
                        .then_inc(A["done"].sem, 1)
            return pe_, act_, dve_, (A["done"], heads)

        mix_stack.close()
        VD = ctx.enter_context(nc.sbuf_tensor("VD", [P, 5900], F32))
        dplace = [0]

        def darea(cols):
            a = dplace[0]
            dplace[0] += cols
            assert dplace[0] <= 5900, dplace[0]
            return VD[:, a:a + cols]

        rot2 = darea(1024).rearrange("p (b t) -> p b t", b=2)
        qk2 = darea(1024).rearrange("p (b t) -> p b t", b=2)
        sm2 = darea(768).rearrange("p (b t) -> p b t", b=2)
        vf2 = darea(512)
        vt2 = darea(512).rearrange("p (c f) -> p c f", c=2)
        zz2 = darea(512)
        yv2 = darea(512)
        rs2 = darea(256)
        sx2 = darea(32)
        lamv = darea(16)
        LAM_INIT = 0.8 - 0.6 * math.exp(-0.3 * 0)

        def diff_phase(name, base, heads, y0, ready):
            names = ("rot:4 t2:2 t1:2 qk:2 s_mm:2 sm:2 mx:4 nm:4 p:4 rc:1 rl:1 pn:4 pd:2 pt_mm:1 pt_ok:1 vf:1 vt_mm:1 "
                     "vt_ok:1 o_mm:1 tz:1 zz:1 sq:1 ms_mm:1 lns:1 rs:1 y1:1 y2:2 yhi:1 done:1 lam=6 lmm=1 lex=1")
            B = counts(name, names, heads)
            mask = cns2[:, CN2["caus"]]

            def pe_(pe):
                ready[0].wait(pe, ready[1])
                B["lam"].wait(pe, 2)
                nc.tensor.matmul(ps[:, 6, 0:2], meanw, lamv[:, 0:2], start=True, stop=True).then_inc(B["lmm"].sem, 1)
                with pe.Fori(0, heads) as i:
                    def tile(k, out):
                        mm_tile(pe, base, i, U_DIFF, k, out, 0)
                    B["t1"].wait(pe, 2 * i)
                    tile(0, ps[:, 0, 0:T])
                    tile(2, ps[:, 0, T:])
                    tile(4, ps[:, 1, 0:T])
                    tile(6, ps[:, 1, T:])
                    tile(8, ps[:, 2, 0:T])
                    B["qk"].wait(pe, 2 * i + 2)
                    for b in range(2):
                        q, k = qk2[:, 0, b * T:b * T + T], qk2[:, 1, b * T:b * T + T]
                        nc.tensor.matmul(ps[:, 4 + b, 0:P], q[:, 0:P], k[:, 0:P], start=True, stop=True)
                        nc.tensor.matmul(ps[:, 4 + b, P:3 * P], q[:, P:], k, start=True, stop=True)\
                            .then_inc(B["s_mm"].sem, 1)
                    tile(10, ps[:, 2, T:])
                    tile(12, ps[:, 3, 0:T])
                    B["vf"].wait(pe, i + 1)
                    for c in range(2):
                        for m in range(2):
                            o = c * T + m * P
                            ins = nc.tensor.transpose(ps[:, 7, o:o + P], vf2[:, m * T + c * P:m * T + c * P + P], ident)
                    ins.then_inc(B["vt_mm"].sem, 1)
                    B["pd"].wait(pe, 2 * i + 2)
                    for c in range(3):
                        ins = nc.tensor.transpose(ps[:, 6, P * c:P * c + P], sm2[:, 0, P * c:P * c + P], ident)
                    ins.then_inc(B["pt_mm"].sem, 1)
                    tile(14, ps[:, 3, T:])
                    B["vt_ok"].wait(pe, i + 1)
                    B["pt_ok"].wait(pe, i + 1)
                    for m in range(2):
                        nc.tensor.matmul(ps[:, 4, m * T:m * T + T], vt2[:, 0, m * P:m * P + P], pt[:, 0:T], start=True,
                                         stop=False)
                        ins = nc.tensor.matmul(ps[:, 4, m * T + P:m * T + T], vt2[:, 1, m * P:m * P + P], pt[:, T:],
                                               start=False, stop=True)
                    ins.then_inc(B["o_mm"].sem, 1)
                    B["sq"].wait(pe, i + 1)
                    for m in range(2):
                        ins = nc.tensor.matmul(ps[:, 5, 0:T], meanw, yv2[:, m * T:m * T + T], start=m == 0, stop=m == 1)
                    ins.then_inc(B["ms_mm"].sem, 1)

            def act_(act):
                B["lmm"].wait(act, 1)
                nc.scalar.activation(lamv[:, 2:4], ps[:, 6, 0:2], ACT.Exp, scale=float(KT * P)).then_inc(B["lex"].sem, 1)
                with act.Fori(0, heads) as i:
                    def hi(*ks):
                        for k in ks:
                            split_hi(act, (base + k + LEAD) % RING, (i, U_DIFF, base + k + LEAD))
                    hi(0, 1, 2, 3, 4)
                    B["t2"].wait(act, 2 * i)
                    for b in range(2):
                        act.wait_ge(unit_used, i * U_DIFF + (base + 4 + 4 * b))
                        for h in range(2):
                            nc.scalar.activation(rot2[64 * h:64 * h + 64, b], ps[64 - 64 * h:128 - 64 * h, b, :], ACT.Copy)\
                                .then_inc(B["rot"].sem, 1)
                        if b == 0:
                            hi(5, 6)
                    hi(7, 8)
                    for b in range(2):
                        for k in range(2):
                            B["nm"].wait(act, 4 * i + 2 * b + k + 1)
                            n = 2 * b + k
                            nc.scalar.activation(rows(sm2[:, b], k), rows(sm2[:, b], k), ACT.Exp, bias=sx2[:, 4 + n:5 + n],
                                                 scale=SC, accum_out=sx2[:, 8 + n:9 + n]).then_inc(B["p"].sem, 1)
                        if b == 0:
                            hi(9)
                    act.wait_ge(unit_used, i * U_DIFF + (base + 12))
                    nc.scalar.activation(vf2, ps[:, 2, :], ACT.Copy).then_inc(B["vf"].sem, 1)
                    hi(10, 11, 12)
                    B["vt_mm"].wait(act, i + 1)
                    nc.scalar.activation(vt2.rearrange("p c f -> p (c f)"), ps[:, 7, :], ACT.Copy)\
                        .then_inc(B["vt_ok"].sem, 1)
                    B["pt_mm"].wait(act, i + 1)
                    nc.scalar.activation(pt, ps[:, 6, 0:3 * P], ACT.Copy).then_inc(B["pt_ok"].sem, 1)
                    act.wait_ge(unit_used, i * U_DIFF + (base + 16))
                    nc.scalar.activation(zz2, ps[:, 3, :], ACT.Tanh, scale=0.5).then_inc(B["tz"].sem, 1)
                    B["o_mm"].wait(act, i + 1)
                    nc.scalar.activation(yv2, ps[:, 4, :], ACT.Square).then_inc(B["sq"].sem, 1)
                    hi(13, 14, 15)
                    B["ms_mm"].wait(act, i + 1)
                    nc.scalar.activation(rs2, ps[:, 5, 0:T], ACT.Ln, bias=kst_[:, 3:4], scale=KT * P / 256.0)\
                        .then_inc(B["lns"].sem, 1)
                    B["lns"].wait(act, i + 1)
                    nc.scalar.activation(rs2, rs2, ACT.Exp, scale=-0.5).then_inc(B["rs"].sem, 1)
                    B["y2"].wait(act, 2 * i + 2)
                    nc.scalar.activation(ahi[:, 1, bass.ds(2 * i + y0, 2), :].rearrange("p a t -> p (a t)"), yv2, ACT.Copy)\
                        .then_inc(B["yhi"].sem, 1)

            def dve_(dve):
                ready[0].wait(dve, ready[1])
                lam4 = pv[:, PV["lam"]]
                for b in range(2):
                    nc.vector.tensor_tensor(lamv[:, b:b + 1], lam4[:, 2 * b:2 * b + 1], lam4[:, 2 * b + 1:2 * b + 2],
                                            ALU.mult).then_inc(B["lam"].sem, 1)
                B["lex"].wait(dve, 1)
                nc.vector.tensor_tensor(lamv[:, 4:5], lamv[:, 3:4], lamv[:, 2:3], ALU.subtract).then_inc(B["lam"].sem, 1)
                B["lam"].wait(dve, 3)
                nc.vector.tensor_scalar(lamv[:, 5:6], lamv[:, 4:5], -LAM_INIT, None, ALU.add).then_inc(B["lam"].sem, 1)
                nc.vector.tensor_scalar(lamv[:, 6:8], pv[:, PV["subln"]], 0.5 * (1.0 - LAM_INIT), None, ALU.mult)\
                    .then_inc(B["lam"].sem, 2)
                B["lam"].wait(dve, 6)
                with dve.Fori(0, heads) as i:
                    for b in range(2):
                        B["rot"].wait(dve, 4 * i + 2 * b + 2)
                        if b == 0:
                            B["done"].wait(dve, i)
                        nc.vector.tensor_tensor(rot2[:, b], rot2[:, b], sin, ALU.mult).then_inc(B["t2"].sem, 1)
                        nc.vector.tensor_tensor(qk2[:, b], ps[:, b, :], cos, ALU.mult).then_inc(B["t1"].sem, 1)
                        B["t1"].wait(dve, 2 * i + b + 1)
                        B["t2"].wait(dve, 2 * i + b + 1)
                        nc.vector.tensor_tensor(qk2[:, b], qk2[:, b], rot2[:, b], ALU.add).then_inc(B["qk"].sem, 1)
                    for b in range(2):
                        B["s_mm"].wait(dve, 2 * i + b + 1)
                        nc.vector.tensor_tensor(sm2[:, b], ps[:, 4 + b, 0:3 * P], mask, ALU.add).then_inc(B["sm"].sem, 1)
                        B["sm"].wait(dve, 2 * i + b + 1)
                        for k in range(2):
                            n = 2 * b + k
                            nc.vector.tensor_reduce(sx2[:, n:n + 1], rows(sm2[:, b], k), AX.X, ALU.max)\
                                .then_inc(B["mx"].sem, 1)
                        for k in range(2):
                            n = 2 * b + k
                            B["mx"].wait(dve, 4 * i + 2 * b + 2)
                            nc.vector.tensor_scalar(sx2[:, 4 + n:5 + n], sx2[:, n:n + 1], -SC, None, ALU.mult)\
                                .then_inc(B["nm"].sem, 1)
                    B["p"].wait(dve, 4 * i + 4)
                    nc.vector.reciprocal(sx2[:, 12:16], sx2[:, 8:12]).then_inc(B["rc"].sem, 1)
                    B["rc"].wait(dve, i + 1)
                    nc.vector.tensor_scalar(sx2[:, 16:18], sx2[:, 14:16], lamv[:, 5:6], None, ALU.mult)\
                        .then_inc(B["rl"].sem, 1)
                    B["rl"].wait(dve, i + 1)
                    for k in range(2):
                        nc.vector.tensor_scalar(rows(sm2[:, 1], k), rows(sm2[:, 1], k), sx2[:, 16 + k:17 + k], None,
                                                ALU.mult).then_inc(B["pn"].sem, 2)
                    B["pn"].wait(dve, 4 * i + 4)
                    for k in range(2):
                        nc.vector.scalar_tensor_tensor(rows(sm2[:, 0], k), rows(sm2[:, 0], k), sx2[:, 12 + k:13 + k],
                                                       rows(sm2[:, 1], k), ALU.mult, ALU.add).then_inc(B["pd"].sem, 1)
                    B["tz"].wait(dve, i + 1)
                    nc.vector.scalar_tensor_tensor(zz2, zz2, 1.0, ps[:, 3, :], ALU.add, ALU.mult).then_inc(B["zz"].sem, 1)
                    B["rs"].wait(dve, i + 1)
                    nc.vector.tensor_tensor(yv2.rearrange("p (m t) -> p m t", m=2),
                                            ps[:, 4, :].rearrange("p (m t) -> p m t", m=2),
                                            rs2.unsqueeze(1).broadcast_to([P, 2, T]), ALU.mult).then_inc(B["y1"].sem, 1)
                    B["y1"].wait(dve, i + 1)
                    B["zz"].wait(dve, i + 1)
                    for m in range(2):
                        half = slice(m * T, m * T + T)
                        nc.vector.scalar_tensor_tensor(yv2[:, half], yv2[:, half], lamv[:, 6 + m:7 + m], zz2[:, half],
                                                       ALU.mult, ALU.mult).then_inc(B["y2"].sem, 1)
                    B["yhi"].wait(dve, i + 1)
                    nsl = bass.ds(2 * i + y0, 2)
                    B["y2"].wait(dve, 2 * i + 2)
                    nc.vector.tensor_tensor(alo[:, 1, nsl, :].rearrange("p a t -> p (a t)"), yv2,
                                            ahi[:, 1, nsl, :].rearrange("p a t -> p (a t)").bitcast(F32), ALU.subtract)\
                        .then_inc(B["done"].sem, 1)
            return pe_, act_, dve_, (B["done"], heads)


        pe_out1, act_out1, pool_out1, dve_out1, out1 = out_phase("out1", S_OUT1, True, mhi, mlo, 0,
                                                            lambda pe, k: M["mlo"].wait(pe, k + 1))
        pe_n1, act_n1, dve_n1, n1 = norm_phase("n1", (out1, KT), "final_g", False, KT)
        pe_n2, act_n2, dve_n2, pool_n2, n2 = norm_phase("n2", n1, "norm_ab", True, KT)
        pe_dil, act_dil, dve_dil, dil = head_phase("dil", S_DIL, 8, "dil", 0, n2)
        pe_diff, act_diff, dve_diff, diff = diff_phase("diff", S_DIFF, 4, 8, dil)
        pe_out2, act_out2, pool_out2, dve_out2, out2 = out_phase("out2", S_OUT2, False, ahi[:, 1], alo[:, 1], 0,
                                                            lambda pe, k: diff[0].wait(pe, max(1, (k - 8) // 2 + 1)))
        pe_n3, act_n3, dve_n3, pool_n3, n3 = norm_phase("n3", (out2, KT), "norm_c", True, KT)
        pe_caus, act_caus, dve_caus, caus = head_phase("caus", S_CAUS, 16, "caus", 0, n3)
        pe_out3, act_out3, pool_out3, dve_out3, out3 = out_phase("out3", S_OUT3, False, ahi[:, 1], alo[:, 1], 0,
                                                            lambda pe, k: caus[0].wait(pe, k + 1))
        pe_n4, act_n4, dve_n4, n4 = norm_phase("n4", (out3, KT), "final_norm", False, KT)
        stored = sem("stored")

        def sp_store(sp):
            for k in range(0, KT, 4):
                n4[0].wait(sp, k + 4)
                sp.dma_start(outT[:, k:k + 4, :], XR[:, k:k + 4, :]).then_inc(stored, 16)
            sp.wait_ge(stored, 64)

        block = ctx.enter_context(nc.Block())

        @block.sync
        def _(sp):
            sp_start(sp)
            open_counts(sp)
            sp_mod(sp)
            sp_stream(sp)
            sp_pairs(sp)
            sp_loop(sp, S_GLA, S_END - S_GLA)
            sp_store(sp)

        @block.gpsimd
        def _(pool):
            pool_h(pool)
            pool_lora(pool)
            pool_pairs(pool)
            pool_gla(pool)
            pool_merge(pool)
            pool_out1(pool)
            pool_n2(pool)
            pool_stream(pool, S_DIL, S_OUT2 - S_DIL)
            pool_out2(pool)
            pool_n3(pool)
            pool_stream(pool, S_CAUS, S_OUT3 - S_CAUS)
            pool_out3(pool)

        @block.scalar
        def _(act):
            act_start(act)
            act_h(act)
            act_lora(act)
            act_pairs(act)
            act_gla(act)
            act_ysplit(act)
            act_merge(act)
            act_out1(act)
            act_n1(act)
            act_n2(act)
            act_dil(act)
            act_diff(act)
            act_out2(act)
            act_n3(act)
            act_caus(act)
            act_out3(act)
            act_n4(act)

        @block.vector
        def _(dve):
            dve_start(dve)
            dve_mod(dve)
            dve_pairs(dve)
            dve_gla(dve)
            dve_ysplit(dve)
            dve_merge(dve)
            M["x_in"].wait(dve, 16)
            M["c_in"].wait(dve, 16)
            dve_out1(dve)
            dve_n1(dve)
            dve_n2(dve)
            dve_dil(dve)
            dve_diff(dve)
            dve_out2(dve)
            dve_n3(dve)
            dve_caus(dve)
            dve_out3(dve)
            dve_n4(dve)

        @block.tensor
        def _(pe):
            pe_mod(pe)
            pe_lora(pe)
            pe_pairs(pe)
            pe_gla(pe)
            pe_merge(pe)
            pe_out1(pe)
            pe_n1(pe)
            pe_n2(pe)
            pe_dil(pe)
            pe_diff(pe)
            pe_out2(pe)
            pe_n3(pe)
            pe_caus(pe)
            pe_out3(pe)
            pe_n4(pe)



def _shape_constants():
    import numpy as np

    cn = np.zeros((P, NCN), np.float32)
    cn[:, CN["ident"]] = np.eye(P)
    cn[:, CN["mean"]] = 1.0 / (KT * P)
    head = np.arange(P) // C
    cn[:, CN["head"]] = head[:, None] == head[None, :]
    tok = np.arange(512)
    keep = np.stack([tok % C != 0, tok % C != C - 1])
    cn[:, CN["keep"]] = keep.reshape(1, -1)
    s = (np.arange(P) % C)[:, None, None]
    t = np.arange(C)[None, None, :]
    back = np.arange(2)[None, :, None]
    earlier = np.where(back == 0, s < t, s > t)
    cn[:, CN["strict"]] = earlier.reshape(P, -1)
    cn[:, CN["incl"]] = (earlier | (s == t)).reshape(P, -1)
    level = [earlier & (s // (2 * m) == t // (2 * m)) & (s // m != t // m) for m in (1, 2, 4, 8, 16, 32)]
    level = np.stack(level, 1)[:, :, :, None, :]
    half = (np.arange(P) // C)[:, None, None, None, None] == np.arange(2)[None, None, None, :, None]
    cn[:, CN["level"]] = (level & half).reshape(P, -1)
    r128 = np.arange(P)
    same = (r128[:, None] // C == r128[None, :] // C)
    cn[:, CN["gmask"]] = np.concatenate([same & (r128[:, None] <= r128[None, :]),
                                         same & (r128[:, None] >= r128[None, :])], 1)
    cn2 = np.zeros((P, NCN2), np.float32)
    half = P // 2
    inv = 1.0 / (10000.0 ** (np.arange(0, P, 2, dtype=np.float32) / np.float32(P))).astype(np.float32)
    ang = (np.arange(T, dtype=np.float32)[None, :] * inv[:, None]).astype(np.float32)
    sign = np.where(np.arange(P) < half, -1.0, 1.0)[:, None]
    cn2[:, CN2["cos"]] = np.tile(np.cos(ang), (2, 2))
    cn2[:, CN2["sin"]] = np.tile(np.sin(ang), (2, 2)) * sign
    q = np.concatenate([np.zeros(P), np.ones(2 * P)])[None, :] * P + np.arange(P)[:, None]
    k = np.concatenate([np.arange(P), np.arange(2 * P)])[None, :]
    rel = q - k
    times = ((rel <= 128) * 1 + (rel % 4 == 0) + (rel % 16 == 0)) * (rel >= 0)
    cn2[:, CN2["dil"]] = np.where(times > 0, np.log(np.maximum(times, 1)) * math.sqrt(P), -1e30)
    cn2[:, CN2["caus"]] = np.where(rel >= 0, 0.0, -1e30)
    return cn, cn2


def kernel(x, c, ctx, c_ctx, w_mod, b_mod, norm_g, w_in, conv_w, a_w0, a_w2, a_a0, a_a2, a_k_k, a_k_a,
           a_r_k, a_lnx_g, a_lnx_b, b_gk_w2, b_gk_b, b_norm_g, w_a, w_b, w_out, final_g, norm_ab_2,
           w_in_ab_2, w_out_ab_2, lam_ab_2, subln_ab_2, norm_c_2, w_in_c_2, w_out_c_2, final_norm_2):
    import numpy as np
    import concourse.bacc as bacc
    from concourse.bass_utils import run_bass_kernel_spmd

    def units(w):
        w = np.asarray(w)
        K, N = w.shape
        return w.reshape(K // 1024, UK, P, N // P, P).transpose(3, 0, 2, 1, 4).reshape(N // P, K // 1024, P, UK * P)

    def woven(*parts):
        parts = [p.reshape(n, -1, P, UK * P) for p, n in parts]
        return np.concatenate(parts, 1).reshape(-1, P, UK * P)

    def feat(v):
        return np.asarray(v).reshape(-1, P).T

    wi = np.asarray(w_in[0])
    lora_g = np.zeros((KT * P, P), np.float32)
    lora_g[:, 0:32] = wi[:, 7424:7456]
    ab, cc = np.asarray(w_in_ab_2[0]), np.asarray(w_in_c_2[0])
    v_b = units(wi[:, 5376:6400]).reshape(GH, 2, 2, P, UK * P)
    stream = np.concatenate([
        units(w_mod[0]).reshape(-1, P, UK * P),
        units(wi[:, 4096:4352]).reshape(-1, P, UK * P), units(lora_g).reshape(-1, P, UK * P),
        woven((units(wi[:, 1024:2048]), 8), (units(wi[:, 0:1024]), 8), (units(wi[:, 2048:3072]), 8),
              (units(wi[:, 3072:4096]), 8)),
        woven((v_b[:, 0], 4), (units(wi[:, 4352:4864]), 4), (units(wi[:, 4864:5376]), 4), (v_b[:, 1], 4),
              (units(wi[:, 6400:7424]), 4)),
        woven((units(wi[:, 7456:9504]), 16), (units(wi[:, 9504:11552]), 16), (units(w_a[0]), 16), (units(w_b[0]), 16)),
        units(w_out[0]).reshape(-1, P, UK * P),
        woven(*[(units(ab[:, a:a + 1024]), 8) for a in (0, 1024, 2048, 6144)]),
        woven(*[(units(ab[:, a:a + 1024]), 4) for a in (3072, 4096, 5120, 7168)]),
        units(w_out_ab_2[0]).reshape(-1, P, UK * P),
        woven(*[(units(cc[:, a:a + 2048]), 16) for a in (0, 2048, 4096, 6144)]),
        units(w_out_c_2[0]).reshape(-1, P, UK * P),
    ])
    xT = np.stack([np.asarray(a)[0].T.reshape(KT, P, T) for a in (x, ctx)]).transpose(2, 0, 1, 3)
    cond = np.stack([np.asarray(c)[0], np.asarray(c_ctx)], 1).reshape(KT, P, 2).transpose(1, 0, 2).reshape(P, 32)
    par = np.concatenate([feat(norm_g[0]), feat(b_mod[0]), feat(final_g), feat(norm_ab_2[0]), feat(norm_c_2[0]),
                          feat(final_norm_2), feat(b_norm_g[0]), feat(subln_ab_2[0]), feat(b_gk_b[0]),
                          feat(lam_ab_2[0]), cond], 1)
    conv = np.asarray(conv_w[0]).reshape(9, 3, PAIRS, P).transpose(3, 2, 1, 0)
    per_pair = [conv[:, :, 1], conv[:, :, 2], conv[:, :, 0]]
    for v in (a_w0[0], a_a0[0]):
        per_pair.append(np.asarray(v).reshape(2, PAIRS, P).transpose(2, 1, 0))
    for v in (a_k_k[0], a_k_a[0], np.asarray(a_r_k[0]).reshape(-1), a_lnx_g[0], a_lnx_b[0]):
        per_pair.append(np.asarray(v).reshape(PAIRS, P, 1).transpose(1, 0, 2))
    for v in (a_w2[0], a_a2[0]):
        per_pair.append(np.asarray(v).reshape(P, PAIRS, P))
    pair_par = np.concatenate(per_pair, 2).transpose(1, 0, 2)
    gk_w = np.zeros((32, 2, 512), np.float32)
    for d in range(2):
        gk_w[16 * d:16 * d + 16, d] = np.asarray(b_gk_w2[0])[d]
    cn, cn2 = _shape_constants()
    arrays = {"stream": stream, "xT": xT, "par": par, "pair_par": pair_par, "gk_w": gk_w, "consts": cn, "consts2": cn2}
    arrays = {k: np.ascontiguousarray(v) for k, v in arrays.items()}
    nc = bacc.Bacc("TRN2", target_bir_lowering=False, num_devices=1)
    args = [nc.dram_tensor(n, a.shape, F32, kind="ExternalInput").ap() for n, a in arrays.items()]
    outT = nc.dram_tensor("outT", (P, KT, T), F32, kind="ExternalOutput").ap()
    build(nc, *args, outT)
    r = run_bass_kernel_spmd(nc, [arrays], core_ids=[0])
    return np.ascontiguousarray(r.results[0]["outT"].transpose(2, 1, 0).reshape(1, T, KT * P))
```
